# Optimizing a Trainium2 kernel written in Bass

```python
import math
import jax
import jax.numpy as jnp
from jax import lax
import numpy as np
import jax, jax.numpy as jnp

D_MODEL = 1024
BATCH = 1
SEQ = 512
DEPTH = 2

N_MIXERS = 4
HEAD_DIM = 64
ROPE_THETA = 500000.0
ROT_DIM = HEAD_DIM // 4
Q_BLOCK = 128

A_HEADS = 16
A_KV_HEADS = 4
A_WINDOW = 128
B_HEADS = 16
B_Q_RANK = 384
B_KV_RANK = 256
B_NOPE = 64
B_ROPE = 32
B_V = 64
C_HEADS = 16
C_KV_HEADS = 4
C_CMP_LEN = 32
C_CMP_STRIDE = 16
C_CMP_HIDDEN = 128
C_SEL_LEN = 64
C_N_SEL = 16
C_WINDOW = 512
D_HEADS = 8
D_SUB = 64
M_GROUPS = 4
M_PER_GROUP = 8
M_EXPERTS = M_GROUPS * M_PER_GROUP
M_TOPK = 2
M_HIDDEN = 512

LN_EPS = 1e-5
RMS_EPS = 1e-6


def layer_norm(x, g, b):
    xf = x.astype(jnp.float32)
    mu = jnp.mean(xf, -1, keepdims=True)
    var = jnp.mean(jnp.square(xf - mu), -1, keepdims=True)
    return ((xf - mu) * lax.rsqrt(var + LN_EPS) * g + b).astype(x.dtype)

def rms_norm(x, g):
    xf = x.astype(jnp.float32)
    return (xf * lax.rsqrt(jnp.mean(jnp.square(xf), -1, keepdims=True) + RMS_EPS) * g).astype(x.dtype)

def rope(x, rot_dim):
    s = x.shape[1]
    half = rot_dim // 2
    inv_freq = 1.0 / (ROPE_THETA ** (jnp.arange(half, dtype=jnp.float32) * (2.0 / rot_dim)))
    ang = jnp.arange(s, dtype=jnp.float32)[:, None] * inv_freq[None, :]
    cos = jnp.cos(ang)[None, :, None, :]
    sin = jnp.sin(ang)[None, :, None, :]
    xr = x[..., :rot_dim].astype(jnp.float32)
    x1, x2 = xr[..., :half], xr[..., half:]
    rot = jnp.concatenate([x1 * cos - x2 * sin, x2 * cos + x1 * sin], -1).astype(x.dtype)
    return jnp.concatenate([rot, x[..., rot_dim:]], -1)

def masked_softmax(s, mask):
    s = jnp.where(mask, s, -jnp.inf)
    m = jnp.max(s, -1, keepdims=True)
    m = jnp.where(jnp.isfinite(m), m, 0.0)
    e = jnp.where(mask, jnp.exp(s - m), 0.0)
    return e / jnp.maximum(jnp.sum(e, -1, keepdims=True), 1e-30)

def causal_attention(q, k, v, scale):
    b, s, h, dq = q.shape
    nb = s // Q_BLOCK
    qb = q.reshape(b, nb, Q_BLOCK, h, dq).transpose(1, 0, 2, 3, 4)
    kpos = jnp.arange(s)

    def block(args):
        qi, blk = args
        sc = jnp.einsum('bqhd,bkhd->bhqk', qi, k).astype(jnp.float32) * scale
        qpos = blk * Q_BLOCK + jnp.arange(Q_BLOCK)
        sc = jnp.where(kpos[None, :] <= qpos[:, None], sc, -jnp.inf)
        p = jax.nn.softmax(sc, axis=-1)
        return jnp.einsum('bhqk,bkhd->bqhd', p.astype(v.dtype), v)

    o = lax.map(block, (qb, jnp.arange(nb)))
    return o.transpose(1, 0, 2, 3, 4).reshape(b, s, h, v.shape[-1])

def swa_sink_gqa(x, w_in, sinks, w_o):
    b, s, _ = x.shape
    g = A_HEADS // A_KV_HEADS
    blk = A_WINDOW
    nb = s // blk
    qd, kd = A_HEADS * HEAD_DIM, A_KV_HEADS * HEAD_DIM
    qkv = x @ w_in
    q = rope(qkv[..., :qd].reshape(b, s, A_HEADS, HEAD_DIM), ROT_DIM)
    k = rope(qkv[..., qd:qd + kd].reshape(b, s, A_KV_HEADS, HEAD_DIM), ROT_DIM)
    v = qkv[..., qd + kd:].reshape(b, s, A_KV_HEADS, HEAD_DIM)
    qb = q.reshape(b, nb, blk, A_KV_HEADS, g, HEAD_DIM)

    def band(t):
        tb = t.reshape(b, nb, blk, A_KV_HEADS, HEAD_DIM)
        prev = jnp.pad(tb, ((0, 0), (1, 0), (0, 0), (0, 0), (0, 0)))[:, :-1]
        return jnp.concatenate([prev, tb], axis=2)

    kb, vb = band(k), band(v)
    sc = jnp.einsum('bnqhgd,bnkhd->bnhgqk', qb, kb).astype(jnp.float32) * HEAD_DIM ** -0.5
    n = jnp.arange(nb)[:, None, None]
    i = jnp.arange(blk)[None, :, None]
    j = jnp.arange(2 * blk)[None, None, :]
    dist = blk + i - j
    mask = (dist >= 0) & (dist < A_WINDOW) & ((n - 1) * blk + j >= 0)
    sc = jnp.where(mask[None, :, None, None], sc, -jnp.inf)
    sink = sinks.astype(jnp.float32).reshape(A_KV_HEADS, g)[None, None, :, :, None, None]
    m = jnp.maximum(jnp.max(sc, -1, keepdims=True), sink)
    e = jnp.exp(sc - m)
    p = e / (jnp.sum(e, -1, keepdims=True) + jnp.exp(sink - m))
    o = jnp.einsum('bnhgqk,bnkhd->bnqhgd', p.astype(vb.dtype), vb)
    return o.reshape(b, s, qd) @ w_o

def mla(x, w_down, q_norm, kv_norm, w_uq, w_ukv, w_o):
    b, s, _ = x.shape
    c = x @ w_down
    cq = rms_norm(c[..., :B_Q_RANK], q_norm)
    ckv = rms_norm(c[..., B_Q_RANK:B_Q_RANK + B_KV_RANK], kv_norm)
    kr = c[..., B_Q_RANK + B_KV_RANK:]
    q = (cq @ w_uq).reshape(b, s, B_HEADS, B_NOPE + B_ROPE)
    q = jnp.concatenate([q[..., :B_NOPE], rope(q[..., B_NOPE:], B_ROPE)], -1)
    kv = (ckv @ w_ukv).reshape(b, s, B_HEADS, B_NOPE + B_V)
    k_rope = rope(kr[:, :, None, :], B_ROPE)
    k = jnp.concatenate([kv[..., :B_NOPE], jnp.broadcast_to(k_rope, (b, s, B_HEADS, B_ROPE))], -1)
    o = causal_attention(q, k, kv[..., B_NOPE:], (B_NOPE + B_ROPE) ** -0.5)
    return o.reshape(b, s, B_HEADS * B_V) @ w_o

def nsa(x, w_in, pos_k, pos_v, wk1, wk2, wv1, wv2, w_o):
    b, s, _ = x.shape
    g = C_HEADS // C_KV_HEADS
    qd, kd = C_HEADS * HEAD_DIM, C_KV_HEADS * HEAD_DIM
    h = x @ w_in
    q = rope(h[..., :qd].reshape(b, s, C_HEADS, HEAD_DIM), ROT_DIM)
    kv = h[..., qd:qd + 6 * kd].reshape(b, s, 6, C_KV_HEADS, HEAD_DIM)
    k_c, v_c = kv[:, :, 0], kv[:, :, 1]
    k_s, v_s = rope(kv[:, :, 2], ROT_DIM), kv[:, :, 3]
    k_w, v_w = rope(kv[:, :, 4], ROT_DIM), kv[:, :, 5]
    gates = jax.nn.sigmoid(h[..., qd + 6 * kd:].astype(jnp.float32)).reshape(b, s, C_HEADS, 3)

    nc = (s - C_CMP_LEN) // C_CMP_STRIDE + 1
    idx = jnp.arange(nc)[:, None] * C_CMP_STRIDE + jnp.arange(C_CMP_LEN)[None, :]

    def compress(t, pe, w1, w2):
        blocks = t[:, idx] + pe[None, None, :, None, :]
        flat = blocks.transpose(0, 1, 3, 2, 4).reshape(b, nc, C_KV_HEADS, C_CMP_LEN * HEAD_DIM)
        return jax.nn.gelu(flat @ w1) @ w2

    k_cmp = compress(k_c, pos_k, wk1, wk2)
    v_cmp = compress(v_c, pos_v, wv1, wv2)
    cmp_start = jnp.arange(nc) * C_CMP_STRIDE
    cmp_end = cmp_start + C_CMP_LEN - 1

    nsb = s // C_SEL_LEN
    n_sel = min(C_N_SEL, nsb)
    sel_start = jnp.arange(nsb) * C_SEL_LEN
    overlap = ((cmp_start[:, None] <= sel_start[None, :] + C_SEL_LEN - 1)
               & (sel_start[None, :] <= cmp_end[:, None])).astype(jnp.float32)
    ks_blk = k_s.reshape(b, nsb, C_SEL_LEN, C_KV_HEADS, HEAD_DIM).transpose(0, 3, 1, 2, 4)
    vs_blk = v_s.reshape(b, nsb, C_SEL_LEN, C_KV_HEADS, HEAD_DIM).transpose(0, 3, 1, 2, 4)
    kw_pad = jnp.pad(k_w, ((0, 0), (C_WINDOW, 0), (0, 0), (0, 0)))
    vw_pad = jnp.pad(v_w, ((0, 0), (C_WINDOW, 0), (0, 0), (0, 0)))

    nqb = s // Q_BLOCK
    qf = q.reshape(b * nqb, Q_BLOCK, C_KV_HEADS, g, HEAD_DIM)
    b_ids = jnp.repeat(jnp.arange(b), nqb)
    blk_ids = jnp.tile(jnp.arange(nqb), b)
    scale = HEAD_DIM ** -0.5
    heads = jnp.arange(C_KV_HEADS)[None, :, None]

    def block(args):
        qi, bi, blk = args
        t = blk * Q_BLOCK + jnp.arange(Q_BLOCK)
        sc = jnp.einsum('qhgd,nhd->qhgn', qi, k_cmp[bi]).astype(jnp.float32) * scale
        p_cmp = masked_softmax(sc, (cmp_end[None, :] <= t[:, None])[:, None, None, :])
        o_cmp = jnp.einsum('qhgn,nhd->qhgd', p_cmp.astype(v_cmp.dtype), v_cmp[bi])
        imp = jnp.einsum('qhgn,nj->qhj', p_cmp, overlap)
        cur = (t // C_SEL_LEN)[:, None, None]
        jb = jnp.arange(nsb)[None, None, :]
        imp = jnp.where((jb == 0) | (jb == cur) | (jb == cur - 1), jnp.inf, imp)
        imp = jnp.where(jb <= cur, imp, -jnp.inf)
        _, sel = lax.top_k(imp, n_sel)
        kg = ks_blk[bi][heads, sel]
        vg = vs_blk[bi][heads, sel].reshape(Q_BLOCK, C_KV_HEADS, n_sel * C_SEL_LEN, HEAD_DIM)
        sc = jnp.einsum('qhgd,qhnld->qhgnl', qi, kg).astype(jnp.float32)
        sc = sc.reshape(Q_BLOCK, C_KV_HEADS, g, n_sel * C_SEL_LEN) * scale
        kpos = (sel[..., None] * C_SEL_LEN + jnp.arange(C_SEL_LEN)).reshape(
            Q_BLOCK, C_KV_HEADS, 1, n_sel * C_SEL_LEN)
        p_slc = masked_softmax(sc, kpos <= t[:, None, None, None])
        o_slc = jnp.einsum('qhgk,qhkd->qhgd', p_slc.astype(vg.dtype), vg)
        kwb = lax.dynamic_slice_in_dim(kw_pad[bi], blk * Q_BLOCK, Q_BLOCK + C_WINDOW, axis=0)
        vwb = lax.dynamic_slice_in_dim(vw_pad[bi], blk * Q_BLOCK, Q_BLOCK + C_WINDOW, axis=0)
        wpos = blk * Q_BLOCK - C_WINDOW + jnp.arange(Q_BLOCK + C_WINDOW)
        dist = t[:, None] - wpos[None, :]
        wmask = (dist >= 0) & (dist < C_WINDOW) & (wpos[None, :] >= 0)
        sc = jnp.einsum('qhgd,khd->qhgk', qi, kwb).astype(jnp.float32) * scale
        p_win = masked_softmax(sc, wmask[:, None, None, :])
        o_win = jnp.einsum('qhgk,khd->qhgd', p_win.astype(vwb.dtype), vwb)
        return jnp.stack([o_cmp, o_slc, o_win], axis=-1)

    o = lax.map(block, (qf, b_ids, blk_ids)).reshape(b, s, C_HEADS, HEAD_DIM, 3)
    o = jnp.sum(o * gates[:, :, :, None, :].astype(o.dtype), axis=-1)
    return o.reshape(b, s, qd) @ w_o

def diff_attention(x, w_in, lq1, lk1, lq2, lk2, subln, w_o, layer_idx):
    b, s, _ = x.shape
    qd = D_HEADS * 2 * D_SUB
    h = x @ w_in
    q = rope(h[..., :qd].reshape(b, s, 2 * D_HEADS, D_SUB), ROT_DIM).reshape(b, s, D_HEADS, 2, D_SUB)
    k = rope(h[..., qd:2 * qd].reshape(b, s, 2 * D_HEADS, D_SUB), ROT_DIM).reshape(b, s, D_HEADS, 2, D_SUB)
    v = h[..., 2 * qd:].reshape(b, s, D_HEADS, 2 * D_SUB)
    lam_init = 0.8 - 0.6 * math.exp(-0.3 * layer_idx)
    lam = (jnp.exp(jnp.sum(lq1.astype(jnp.float32) * lk1.astype(jnp.float32)))
           - jnp.exp(jnp.sum(lq2.astype(jnp.float32) * lk2.astype(jnp.float32))) + lam_init)
    nb = s // Q_BLOCK
    qb = q.reshape(b, nb, Q_BLOCK, D_HEADS, 2, D_SUB).transpose(1, 0, 2, 3, 4, 5)
    kpos = jnp.arange(s)
    scale = D_SUB ** -0.5

    def block(args):
        qi, blk = args
        sc = jnp.einsum('bqhcd,bkhcd->cbhqk', qi, k).astype(jnp.float32) * scale
        qpos = blk * Q_BLOCK + jnp.arange(Q_BLOCK)
        sc = jnp.where(kpos[None, :] <= qpos[:, None], sc, -jnp.inf)
        p = jax.nn.softmax(sc, axis=-1)
        a = p[0] - lam * p[1]
        return jnp.einsum('bhqk,bkhe->bqhe', a.astype(v.dtype), v)

    o = lax.map(block, (qb, jnp.arange(nb))).transpose(1, 0, 2, 3, 4).reshape(b, s, D_HEADS, 2 * D_SUB)
    o = rms_norm(o, subln) * (1.0 - lam_init)
    return o.reshape(b, s, qd) @ w_o

def hier_moe(x, w_group, w_expert, w_gate, w_up, w_down):
    b, s, d = x.shape
    n_tok = b * s
    xt = x.reshape(n_tok, d)
    p_group = jax.nn.softmax((xt @ w_group).astype(jnp.float32), axis=-1)
    g_w, g_idx = lax.top_k(p_group, 1)
    e_logits = (xt @ w_expert).astype(jnp.float32).reshape(n_tok, M_GROUPS, M_PER_GROUP)
    e_logits = e_logits[jnp.arange(n_tok), g_idx[:, 0]]
    e_w, e_idx = lax.top_k(jax.nn.softmax(e_logits, axis=-1), M_TOPK)
    weight = g_w * e_w / jnp.sum(e_w, -1, keepdims=True)
    expert = (g_idx * M_PER_GROUP + e_idx).reshape(-1)
    token = jnp.repeat(jnp.arange(n_tok), M_TOPK)
    order = jnp.argsort(expert)
    tok_sorted = token[order]
    sizes = jnp.bincount(expert, length=M_EXPERTS).astype(jnp.int32)
    xs = xt[tok_sorted]
    hid = jax.nn.silu(lax.ragged_dot(xs, w_gate, sizes)) * lax.ragged_dot(xs, w_up, sizes)
    ys = lax.ragged_dot(hid, w_down, sizes) * weight.reshape(-1)[order][:, None].astype(x.dtype)
    return jax.ops.segment_sum(ys, tok_sorted, num_segments=n_tok).reshape(b, s, d)

def first_inputs(seed: int = 0) -> dict:
    key = jax.random.key(seed)
    keys = iter(jax.random.split(key, 40))
    beta = (8 * DEPTH) ** -0.25
    n_a, n_b, n_c, n_d = (len(range(m, DEPTH, N_MIXERS)) for m in range(N_MIXERS))
    d = D_MODEL

    def normal(shape, scale):
        return jax.random.normal(next(keys), shape, jnp.float32) * scale

    def gain(shape):
        return 1.0 + normal(shape, 0.05)

    a_cols = (A_HEADS + 2 * A_KV_HEADS) * HEAD_DIM
    b_cols = B_Q_RANK + B_KV_RANK + B_ROPE
    c_cols = (C_HEADS + 6 * C_KV_HEADS) * HEAD_DIM + 3 * C_HEADS
    d_cols = 3 * D_HEADS * 2 * D_SUB
    cmp_in = C_CMP_LEN * HEAD_DIM
    return {
        'x': normal((BATCH, SEQ, d), 1.0),
        'a_w_in': normal((n_a, d, a_cols), d ** -0.5),
        'a_sinks': normal((n_a, A_HEADS), 1.0),
        'a_w_o': normal((n_a, A_HEADS * HEAD_DIM, d), (A_HEADS * HEAD_DIM) ** -0.5 * beta),
        'b_w_down': normal((n_b, d, b_cols), d ** -0.5),
        'b_q_norm': gain((n_b, B_Q_RANK)),
        'b_kv_norm': gain((n_b, B_KV_RANK)),
        'b_w_uq': normal((n_b, B_Q_RANK, B_HEADS * (B_NOPE + B_ROPE)), B_Q_RANK ** -0.5),
        'b_w_ukv': normal((n_b, B_KV_RANK, B_HEADS * (B_NOPE + B_V)), B_KV_RANK ** -0.5),
        'b_w_o': normal((n_b, B_HEADS * B_V, d), (B_HEADS * B_V) ** -0.5 * beta),
        'c_w_in': normal((n_c, d, c_cols), d ** -0.5),
        'c_pos_k': normal((n_c, C_CMP_LEN, HEAD_DIM), 0.1),
        'c_pos_v': normal((n_c, C_CMP_LEN, HEAD_DIM), 0.1),
        'c_wk1': normal((n_c, cmp_in, C_CMP_HIDDEN), cmp_in ** -0.5),
        'c_wk2': normal((n_c, C_CMP_HIDDEN, HEAD_DIM), C_CMP_HIDDEN ** -0.5),
        'c_wv1': normal((n_c, cmp_in, C_CMP_HIDDEN), cmp_in ** -0.5),
        'c_wv2': normal((n_c, C_CMP_HIDDEN, HEAD_DIM), C_CMP_HIDDEN ** -0.5),
        'c_w_o': normal((n_c, C_HEADS * HEAD_DIM, d), (C_HEADS * HEAD_DIM) ** -0.5 * beta),
        'd_w_in': normal((n_d, d, d_cols), d ** -0.5),
        'd_lq1': normal((n_d, D_SUB), 0.1),
        'd_lk1': normal((n_d, D_SUB), 0.1),
        'd_lq2': normal((n_d, D_SUB), 0.1),
        'd_lk2': normal((n_d, D_SUB), 0.1),
        'd_subln': gain((n_d, 2 * D_SUB)),
        'd_w_o': normal((n_d, D_HEADS * 2 * D_SUB, d), (D_HEADS * 2 * D_SUB) ** -0.5 * beta),
        'moe_w_group': normal((DEPTH, d, M_GROUPS), d ** -0.5),
        'moe_w_expert': normal((DEPTH, d, M_EXPERTS), d ** -0.5),
        'moe_w_gate': normal((DEPTH, M_EXPERTS, d, M_HIDDEN), d ** -0.5),
        'moe_w_up': normal((DEPTH, M_EXPERTS, d, M_HIDDEN), d ** -0.5),
        'moe_w_down': normal((DEPTH, M_EXPERTS, M_HIDDEN, d), M_HIDDEN ** -0.5 * beta),
        'ln_g': gain((DEPTH, 2, d)),
        'ln_b': normal((DEPTH, 2, d), 0.02),
    }

def first_block(x, a_w_in, a_sinks, a_w_o,
              b_w_down, b_q_norm, b_kv_norm, b_w_uq, b_w_ukv, b_w_o,
              c_w_in, c_pos_k, c_pos_v, c_wk1, c_wk2, c_wv1, c_wv2, c_w_o,
              d_w_in, d_lq1, d_lk1, d_lq2, d_lk2, d_subln, d_w_o,
              moe_w_group, moe_w_expert, moe_w_gate, moe_w_up, moe_w_down,
              ln_g, ln_b):
    alpha = (2 * DEPTH) ** 0.25
    h = x
    for i in range(DEPTH):
        kind, j = i % N_MIXERS, i // N_MIXERS
        if kind == 0:
            y = swa_sink_gqa(h, a_w_in[j], a_sinks[j], a_w_o[j])
        elif kind == 1:
            y = mla(h, b_w_down[j], b_q_norm[j], b_kv_norm[j], b_w_uq[j], b_w_ukv[j], b_w_o[j])
        elif kind == 2:
            y = nsa(h, c_w_in[j], c_pos_k[j], c_pos_v[j], c_wk1[j], c_wk2[j], c_wv1[j], c_wv2[j], c_w_o[j])
        else:
            y = diff_attention(h, d_w_in[j], d_lq1[j], d_lk1[j], d_lq2[j], d_lk2[j], d_subln[j], d_w_o[j], i)
        h = layer_norm(alpha * h + y, ln_g[i, 0], ln_b[i, 0])
        y = hier_moe(h, moe_w_group[i], moe_w_expert[i], moe_w_gate[i], moe_w_up[i], moe_w_down[i])
        h = layer_norm(alpha * h + y, ln_g[i, 1], ln_b[i, 1])
    return h


CTX_LEN = 256
GRID_W = 64
EPS = 1e-6
NEG_INF = -1e30

GLA_HEADS = 6
GLA_DK = 32
GLA_DV = 64
GLA_LOWRANK = 16
GLA_TAU = 16.0
GLA_CHUNK = 16
ROPE_BASE = 10000.0
SC_WIDTH = 256
SC_GROUPS = 4
NA_HEADS = 6
NA_DH = 64
NA_WIN_ROWS = 8
NA_WIN_COLS = 16
FFN_DIM = 2816

GLA_QK = GLA_HEADS * GLA_DK
GLA_V = GLA_HEADS * GLA_DV
NA_W = NA_HEADS * NA_DH
MIX_WIDTH = GLA_V + SC_WIDTH + NA_W
IN_SPLIT = (GLA_QK, GLA_QK, GLA_V, GLA_LOWRANK, GLA_LOWRANK, GLA_V,
            SC_WIDTH, SC_WIDTH, SC_WIDTH, NA_W, NA_W, NA_W)
IN_WIDTH = 2 * GLA_QK + 2 * GLA_V + 2 * GLA_LOWRANK + 3 * SC_WIDTH + 3 * NA_W


def rmsnorm(t, g):
    tf = t.astype(jnp.float32)
    y = tf * lax.rsqrt(jnp.mean(tf * tf, axis=-1, keepdims=True) + EPS)
    return (y * g.astype(jnp.float32)).astype(t.dtype)

def modulate(t, shift, scale):
    return t * (1 + scale) + shift

def split_cols(u):
    parts, start = [], 0
    for size in IN_SPLIT:
        parts.append(u[..., start:start + size])
        start += size
    return parts

def dwconv3(t, w, b):
    tp = jnp.pad(t, ((0, 0), (1, 1), (0, 0)))
    return tp[:, :-2] * w[0] + tp[:, 1:-1] * w[1] + tp[:, 2:] * w[2] + b

def axial_rope(n_tokens, dim):
    t = jnp.arange(n_tokens)
    n_freq = dim // 4
    inv_freq = ROPE_BASE ** (-jnp.arange(n_freq, dtype=jnp.float32) / n_freq)
    row = (t // GRID_W).astype(jnp.float32)[:, None] * inv_freq
    col = (t % GRID_W).astype(jnp.float32)[:, None] * inv_freq
    ang = jnp.concatenate([row, col], axis=-1)
    return jnp.cos(ang)[None, :, None, :], jnp.sin(ang)[None, :, None, :]

def apply_rope(t, cos, sin):
    t1, t2 = t[..., 0::2], t[..., 1::2]
    return jnp.stack([t1 * cos - t2 * sin, t1 * sin + t2 * cos], axis=-1).reshape(t.shape)

def gla_chunked(q, k, v, g, s0):
    bsz, n_tok, h, dk = q.shape
    dv = v.shape[-1]
    n_chunks = n_tok // GLA_CHUNK
    rs = lambda t: t.reshape(bsz, n_chunks, GLA_CHUNK, h, t.shape[-1])
    q, k, v, g = rs(q), rs(k), rs(v), rs(g)
    b = jnp.cumsum(g, axis=2)
    b_last = b[:, :, -1:]
    q_dec = q * jnp.exp(b)
    k_inv = k * jnp.exp(-b)
    k_end = k * jnp.exp(b_last - b)
    causal = jnp.tril(jnp.ones((GLA_CHUNK, GLA_CHUNK), dtype=bool))
    a = jnp.einsum('bnihk,bnjhk->bnhij', q_dec, k_inv)
    a = jnp.where(causal, a, 0.0)
    o_intra = jnp.einsum('bnhij,bnjhv->bnihv', a, v)

    def step(s, xs):
        qd, ke, vv, dec = xs
        o = jnp.einsum('bihk,bhkv->bihv', qd, s)
        s = s * dec[..., None] + jnp.einsum('bjhk,bjhv->bhkv', ke, vv)
        return s, o

    xs = (jnp.moveaxis(q_dec, 1, 0), jnp.moveaxis(k_end, 1, 0), jnp.moveaxis(v, 1, 0),
          jnp.moveaxis(jnp.exp(b_last[:, :, 0]), 1, 0))
    s_final, o_inter = lax.scan(step, s0, xs)
    o = o_intra + jnp.moveaxis(o_inter, 0, 1)
    return o.reshape(bsz, n_tok, h, dv), s_final

def gla_prep(q, k, v, glr_f, glr_b, wg2_fw, bg_fw, wg2_bw, bg_bw, rope):
    bsz, n_tok, _ = q.shape
    heads = lambda t, d: t.astype(jnp.float32).reshape(bsz, n_tok, GLA_HEADS, d)
    q = heads(q, GLA_DK) * (GLA_DK ** -0.5)
    k = heads(k, GLA_DK)
    v = heads(v, GLA_DV)
    if rope is not None:
        q = apply_rope(q, rope[0], rope[1])
        k = apply_rope(k, rope[0], rope[1])
    g_f = heads(jax.nn.log_sigmoid((glr_f @ wg2_fw + bg_fw).astype(jnp.float32)), GLA_DK) / GLA_TAU
    g_b = heads(jax.nn.log_sigmoid((glr_b @ wg2_bw + bg_bw).astype(jnp.float32)), GLA_DK) / GLA_TAU
    return q, k, v, g_f, g_b

def gla_output(o, r, norm_g):
    of = o * lax.rsqrt(jnp.mean(o * o, axis=-1, keepdims=True) + EPS) * norm_g.astype(jnp.float32)
    bsz, n_tok = o.shape[:2]
    return (of.reshape(bsz, n_tok, GLA_V) * jax.nn.silu(r.astype(jnp.float32))).astype(r.dtype)

def gla_mixer(lat, cpar, rope, wg2_fw, bg_fw, wg2_bw, bg_bw, norm_g, need_ctx_out):
    flip = lambda t: jnp.flip(t, axis=1)
    qc, kc, vc, gfc, gbc = gla_prep(*cpar[:5], wg2_fw, bg_fw, wg2_bw, bg_bw, None)
    ql, kl, vl, gfl, gbl = gla_prep(*lat[:5], wg2_fw, bg_fw, wg2_bw, bg_bw, rope)
    s0 = jnp.zeros((qc.shape[0], GLA_HEADS, GLA_DK, GLA_DV), jnp.float32)
    oc_f, sc_f = gla_chunked(qc, kc, vc, gfc, s0)
    oc_b, sc_b = gla_chunked(flip(qc), flip(kc), flip(vc), flip(gbc), s0)
    ol_f, _ = gla_chunked(ql, kl, vl, gfl, sc_f)
    ol_b, _ = gla_chunked(flip(ql), flip(kl), flip(vl), flip(gbl), sc_b)
    out_lat = gla_output(ol_f + flip(ol_b), lat[5], norm_g)
    out_ctx = gla_output(oc_f + flip(oc_b), cpar[5], norm_g) if need_ctx_out else None
    return out_lat, out_ctx

def short_conv(b_gate, c_gate, xh, w, bias):
    return b_gate * dwconv3(c_gate * xh, w, bias)

def neighbourhood_attention(q, k, v, k_ctx, v_ctx, rpb):
    bsz, n_tok, _ = q.shape
    rows = n_tok // GRID_W
    kh = min(NA_WIN_ROWS, rows)
    kw = NA_WIN_COLS
    grid = lambda t: t.reshape(bsz, rows, GRID_W, NA_HEADS, NA_DH)
    qg = grid(q.astype(jnp.float32) * (NA_DH ** -0.5))
    kg, vg = grid(k), grid(v)
    kc = k_ctx.reshape(bsz, -1, NA_HEADS, NA_DH).astype(jnp.float32)
    vc = v_ctx.reshape(bsz, -1, NA_HEADS, NA_DH).astype(jnp.float32)
    col = jnp.arange(GRID_W)
    col_start = jnp.clip(col - kw // 2, 0, GRID_W - kw)
    col_mask = (col[None, :] >= col_start[:, None]) & (col[None, :] < col_start[:, None] + kw)
    dc_idx = jnp.clip(col[None, :] - col[:, None] + NA_WIN_COLS - 1, 0, 2 * NA_WIN_COLS - 2)
    rpb_cols = jnp.take(rpb.astype(jnp.float32), dc_idx, axis=2)

    def row_block(r):
        rs = jnp.clip(r - kh // 2, 0, rows - kh)
        q_r = lax.dynamic_index_in_dim(qg, r, axis=1, keepdims=False)
        k_band = lax.dynamic_slice_in_dim(kg, rs, kh, axis=1).astype(jnp.float32)
        v_band = lax.dynamic_slice_in_dim(vg, rs, kh, axis=1).astype(jnp.float32)
        dr_idx = rs + jnp.arange(kh) - r + NA_WIN_ROWS - 1
        bias = jnp.take(rpb_cols, dr_idx, axis=1)
        s_loc = jnp.einsum('bqhd,bikhd->bhqik', q_r, k_band) + jnp.transpose(bias, (0, 2, 1, 3))[None]
        s_loc = jnp.where(col_mask[None, None, :, None, :], s_loc, NEG_INF)
        s_ctx = jnp.einsum('bqhd,bchd->bhqc', q_r, kc)
        s = jnp.concatenate([s_loc.reshape(bsz, NA_HEADS, GRID_W, kh * GRID_W), s_ctx], axis=-1)
        p = jax.nn.softmax(s, axis=-1)
        p_loc = p[..., :kh * GRID_W].reshape(bsz, NA_HEADS, GRID_W, kh, GRID_W)
        p_ctx = p[..., kh * GRID_W:]
        o = jnp.einsum('bhqik,bikhd->bqhd', p_loc, v_band) + jnp.einsum('bhqc,bchd->bqhd', p_ctx, vc)
        return o.astype(q.dtype)

    out = lax.map(row_block, jnp.arange(rows))
    return jnp.moveaxis(out, 0, 1).reshape(bsz, n_tok, NA_W)

def context_attention(q, k, v):
    bsz, n_tok, _ = q.shape
    hs = lambda t: t.astype(jnp.float32).reshape(bsz, n_tok, NA_HEADS, NA_DH)
    s = jnp.einsum('bqhd,bkhd->bhqk', hs(q) * (NA_DH ** -0.5), hs(k))
    o = jnp.einsum('bhqk,bkhd->bqhd', jax.nn.softmax(s, axis=-1), hs(v))
    return o.reshape(bsz, n_tok, NA_W).astype(q.dtype)

def conv_ffn(h, w_up, cw, cb, w_down):
    u = dwconv3(h @ w_up, cw, cb)
    a, b = jnp.split(u, 2, axis=-1)
    return (jax.nn.silu(a) * b) @ w_down

def second_inputs(seed: int = 0) -> dict:
    key = jax.random.key(seed)
    ks = jax.random.split(key, 24)
    nrm = lambda k, shape, s: jax.random.normal(k, shape, jnp.float32) * s
    return {
        "x": nrm(ks[0], (BATCH, SEQ, D_MODEL), 1.0),
        "c": nrm(ks[1], (BATCH, D_MODEL), 1.0),
        "ctx": nrm(ks[2], (BATCH, CTX_LEN, D_MODEL), 1.0),
        "c_ctx": nrm(ks[3], (D_MODEL,), 1.0),
        "w_ada": nrm(ks[4], (DEPTH, D_MODEL, 6 * D_MODEL), 0.5 * D_MODEL ** -0.5),
        "b_ada": nrm(ks[5], (DEPTH, 6 * D_MODEL), 0.02),
        "norm_mix_g": 1.0 + nrm(ks[6], (DEPTH, D_MODEL), 0.05),
        "norm_ffn_g": 1.0 + nrm(ks[7], (DEPTH, D_MODEL), 0.05),
        "w_in": nrm(ks[8], (DEPTH, D_MODEL, IN_WIDTH), D_MODEL ** -0.5),
        "gla_wg2_fw": nrm(ks[9], (DEPTH, GLA_LOWRANK, GLA_QK), GLA_LOWRANK ** -0.5),
        "gla_bg_fw": nrm(ks[10], (DEPTH, GLA_QK), 0.02),
        "gla_wg2_bw": nrm(ks[11], (DEPTH, GLA_LOWRANK, GLA_QK), GLA_LOWRANK ** -0.5),
        "gla_bg_bw": nrm(ks[12], (DEPTH, GLA_QK), 0.02),
        "gla_norm_g": 1.0 + nrm(ks[13], (DEPTH, GLA_DV), 0.05),
        "sc_conv_w": nrm(ks[14], (DEPTH, 3, SC_WIDTH), 3 ** -0.5),
        "sc_conv_b": nrm(ks[15], (DEPTH, SC_WIDTH), 0.02),
        "na_rpb": nrm(ks[16], (DEPTH, NA_HEADS, 2 * NA_WIN_ROWS - 1, 2 * NA_WIN_COLS - 1), 0.02),
        "w_out": nrm(ks[17], (DEPTH, MIX_WIDTH, D_MODEL), MIX_WIDTH ** -0.5),
        "ffn_w_up": nrm(ks[18], (DEPTH, D_MODEL, 2 * FFN_DIM), D_MODEL ** -0.5),
        "ffn_conv_w": nrm(ks[19], (DEPTH, 3, 2 * FFN_DIM), 3 ** -0.5),
        "ffn_conv_b": nrm(ks[20], (DEPTH, 2 * FFN_DIM), 0.02),
        "ffn_w_down": nrm(ks[21], (DEPTH, FFN_DIM, D_MODEL), FFN_DIM ** -0.5),
        "final_norm_g": 1.0 + nrm(ks[22], (D_MODEL,), 0.05),
    }

def second_block(x, c, ctx, c_ctx, w_ada, b_ada, norm_mix_g, norm_ffn_g, w_in, gla_wg2_fw, gla_bg_fw,
              gla_wg2_bw, gla_bg_bw, gla_norm_g, sc_conv_w, sc_conv_b, na_rpb, w_out, ffn_w_up,
              ffn_conv_w, ffn_conv_b, ffn_w_down, final_norm_g):
    n_lat = x.shape[1]
    rope = axial_rope(n_lat, GLA_DK)
    xc = ctx
    for layer in range(DEPTH):
        update_ctx = layer < DEPTH - 1
        mod = jax.nn.silu(c) @ w_ada[layer] + b_ada[layer]
        sh1, sc1, g1, sh2, sc2, g2 = jnp.split(mod[:, None, :], 6, axis=-1)
        modc = jax.nn.silu(c_ctx) @ w_ada[layer] + b_ada[layer]
        sh1c, sc1c, g1c, sh2c, sc2c, g2c = jnp.split(modc, 6, axis=-1)

        u = modulate(rmsnorm(x, norm_mix_g[layer]), sh1, sc1) @ w_in[layer]
        uc = modulate(rmsnorm(xc, norm_mix_g[layer]), sh1c, sc1c) @ w_in[layer]
        lat = split_cols(u)
        cpar = split_cols(uc)
        gla_lat, gla_ctx = gla_mixer(lat[:6], cpar[:6], rope, gla_wg2_fw[layer], gla_bg_fw[layer],
                                     gla_wg2_bw[layer], gla_bg_bw[layer], gla_norm_g[layer], update_ctx)
        sc_lat = short_conv(lat[6], lat[7], lat[8], sc_conv_w[layer], sc_conv_b[layer])
        na_lat = neighbourhood_attention(lat[9], lat[10], lat[11], cpar[10], cpar[11], na_rpb[layer])
        x = x + g1 * (jnp.concatenate([gla_lat, sc_lat, na_lat], axis=-1) @ w_out[layer])
        h = modulate(rmsnorm(x, norm_ffn_g[layer]), sh2, sc2)
        x = x + g2 * conv_ffn(h, ffn_w_up[layer], ffn_conv_w[layer], ffn_conv_b[layer], ffn_w_down[layer])

        if update_ctx:
            sc_ctx = short_conv(cpar[6], cpar[7], cpar[8], sc_conv_w[layer], sc_conv_b[layer])
            na_ctx = context_attention(cpar[9], cpar[10], cpar[11])
            xc = xc + g1c * (jnp.concatenate([gla_ctx, sc_ctx, na_ctx], axis=-1) @ w_out[layer])
            hc = modulate(rmsnorm(xc, norm_ffn_g[layer]), sh2c, sc2c)
            xc = xc + g2c * conv_ffn(hc, ffn_w_up[layer], ffn_conv_w[layer], ffn_conv_b[layer],
                                     ffn_w_down[layer])
    return rmsnorm(x, final_norm_g)


def setup_inputs(seed=0):
    out = dict(first_inputs(seed))
    for name, value in second_inputs(seed + 1).items():
        if name != "x":
            out[name + "_2"] = value
    return out


def reference(
    x, a_w_in, a_sinks, a_w_o, b_w_down, b_q_norm, b_kv_norm, b_w_uq, b_w_ukv, b_w_o, c_w_in,
    c_pos_k, c_pos_v, c_wk1, c_wk2, c_wv1, c_wv2, c_w_o, d_w_in, d_lq1, d_lk1, d_lq2, d_lk2,
    d_subln, d_w_o, moe_w_group, moe_w_expert, moe_w_gate, moe_w_up, moe_w_down, ln_g, ln_b,
    c_2, ctx_2, c_ctx_2, w_ada_2, b_ada_2, norm_mix_g_2, norm_ffn_g_2, w_in_2, gla_wg2_fw_2,
    gla_bg_fw_2, gla_wg2_bw_2, gla_bg_bw_2, gla_norm_g_2, sc_conv_w_2, sc_conv_b_2, na_rpb_2,
    w_out_2, ffn_w_up_2, ffn_conv_w_2, ffn_conv_b_2, ffn_w_down_2, final_norm_g_2,
):
    x = first_block(
        x, a_w_in, a_sinks, a_w_o, b_w_down, b_q_norm, b_kv_norm, b_w_uq, b_w_ukv, b_w_o,
        c_w_in, c_pos_k, c_pos_v, c_wk1, c_wk2, c_wv1, c_wv2, c_w_o, d_w_in, d_lq1, d_lk1,
        d_lq2, d_lk2, d_subln, d_w_o, moe_w_group, moe_w_expert, moe_w_gate, moe_w_up,
        moe_w_down, ln_g, ln_b,
    )
    return second_block(
        x, c_2, ctx_2, c_ctx_2, w_ada_2, b_ada_2, norm_mix_g_2, norm_ffn_g_2, w_in_2,
        gla_wg2_fw_2, gla_bg_fw_2, gla_wg2_bw_2, gla_bg_bw_2, gla_norm_g_2, sc_conv_w_2,
        sc_conv_b_2, na_rpb_2, w_out_2, ffn_w_up_2, ffn_conv_w_2, ffn_conv_b_2, ffn_w_down_2,
        final_norm_g_2,
    )


_drawn_inputs = setup_inputs


def setup_inputs(seed=0):
    import zlib

    import numpy as np

    out = dict(_drawn_inputs(seed))
    spreads = {}
    factors = {'a_sinks': 6.532,
     'b_q_norm': 8.0,
     'b_kv_norm': 7.293,
     'gla_wg2_fw_2': 2.717,
     'gla_bg_fw_2': 8.0,
     'gla_wg2_bw_2': 2.858,
     'gla_bg_bw_2': 8.0,
     'gla_norm_g_2': 6.408,
     'sc_conv_b_2': 8.0,
     'na_rpb_2': 64.0,
     'ffn_conv_b_2': 7.059,
     'norm_ffn_g_2': 2.954}
    for name, (base, spread) in spreads.items():
        noise = np.random.default_rng([zlib.crc32(name.encode()), seed]).standard_normal(out[name].shape)
        drawn = base * np.exp(spread * noise) if base else spread * noise
        out[name] = jnp.asarray(drawn.astype(out[name].dtype))
    for name, factor in factors.items():
        out[name] = (out[name] * factor).astype(out[name].dtype)
    return out
```

```python
import math
from contextlib import ExitStack

import numpy as np

import concourse.bass as bass
from concourse import mybir

F32 = mybir.dt.float32
F32R = mybir.dt.float32r
I32 = mybir.dt.int32
ALU = mybir.AluOpType
ACT = mybir.ActivationFunctionType
AX_X = mybir.AxisListType.X

P = 128
DM = 1024
KD = DM // P
T = 512
NT = T // P
TC = 256
NTC = TC // P
NTT = NT + NTC
BANK = 512
NEG = -1e30

DEPTH = 2
ALPHA = (2 * DEPTH) ** 0.25
LN_EPS = 1e-5
RMS_EPS = 1e-6

DH = 64
A_HEADS, A_KV, A_ROT = 16, 4, 8
B_HEADS, B_QR, B_KVR, B_NOPE, B_ROPE, B_V = 16, 384, 256, 64, 32, 64
B_DQ = B_NOPE + B_ROPE
B_DOWN = B_QR + B_KVR + B_ROPE

GROUPS, PER_GROUP, EXPERTS, HID = 4, 8, 32, 512
SENTINEL = 1 << 20

GLA_H, GLA_DK, GLA_DV, GLA_LR, CHUNK, GLA_TAU = 6, 32, 64, 16, 16, 16.0
QK = GLA_H * GLA_DK
GV = GLA_H * GLA_DV
NCH = (T + TC) // CHUNK
HG = 3
NA_H = 6
GRID_W, NA_WIN = 64, 16
FFN = 2816
NF = FFN // P



def constant_columns():
    p = np.arange(P)
    j, i = p[:, None], p[None, :]
    same = (j // CHUNK) == (i // CHUNK)
    parts = {}
    parts["ident"] = np.eye(P)
    parts["ones"] = np.ones((P, P))
    parts["before"] = (j < i) * 1.0
    causal = np.where(i <= j, 0.0, NEG)
    parts["causal"] = np.concatenate([np.zeros((P, T - P)), causal], 1)
    parts["window"] = np.concatenate([np.where(i > j, 0.0, NEG), causal], 1)
    parts["upto"] = (same & (j <= i)) * 1.0
    parts["from"] = (same & (j >= i)) * 1.0
    parts["sum_upto"] = (same & (j <= i)) / GLA_TAU
    parts["sum_after"] = (same & (j > i)) / GLA_TAU
    parts["sum_from"] = (same & (j >= i)) / GLA_TAU
    parts["sum_before"] = (same & (j < i)) / GLA_TAU
    chunk = (j // CHUNK == np.arange(P // CHUNK)[None, :]) * 1.0
    parts["chunk"] = chunk
    parts["chunk_tau"] = chunk / GLA_TAU
    parts["experts"] = np.broadcast_to(np.arange(EXPERTS)[None, :], (P, EXPERTS)) * 1.0
    tok = np.arange(NT)[None, :] * P + p[:, None]
    parts["assignment"] = (2 * tok[:, :, None] + np.arange(2)).reshape(P, -1) * 1.0
    col = p % GRID_W
    start = np.clip(col - NA_WIN // 2, 0, GRID_W - NA_WIN)
    key = np.arange(GRID_W)[None, :]
    parts["columns"] = np.where((key >= start[:, None]) & (key < start[:, None] + NA_WIN), 0.0, NEG)

    def table(name, ang):
        parts[name + "_cos"] = np.cos(ang).reshape(P, -1)
        parts[name + "_sin"] = np.sin(ang).reshape(P, -1)

    f32 = np.float32
    for name, rot in (("rope_a", 2 * A_ROT), ("rope_b", B_ROPE)):
        inv = (1.0 / (f32(500000.0) ** (np.arange(rot // 2, dtype=f32) * f32(2.0 / rot)))).astype(f32)
        table(name, tok[:, :, None].astype(f32) * inv)
    nf = GLA_DK // 4
    inv = (f32(10000.0) ** (-np.arange(nf, dtype=f32) / nf)).astype(f32)
    row, c = (tok // GRID_W).astype(f32), (tok % GRID_W).astype(f32)
    table("rope_g", np.concatenate([row[:, :, None] * inv, c[:, :, None] * inv], -1))
    at, cols = {}, 0
    for name, a in parts.items():
        at[name] = (cols, a.shape[1])
        cols += a.shape[1]
    return at, np.concatenate([a.astype(np.float32) for a in parts.values()], 1)


class Order:

    def __init__(self, eng, sem):
        self.eng, self.sem, self.n = eng, sem, 0

    def done(self, ins):
        self.n += 1
        ins.then_inc(self.sem, 1)
        self.eng.wait_ge(self.sem, self.n)


class Program:
    def __init__(self, nc, ins, out):
        self.nc, self.ins, self.out = nc, ins, out
        self.uid = 0

    class Sems:
        def __init__(self, prog, phase):
            self.prog, self.phase, self.all = prog, phase, []

        def __call__(self, name):
            s = self.prog.nc.alloc_semaphore(f"{self.phase}_{name}_{self.prog.uid}")
            self.prog.uid += 1
            self.all.append(s)
            return s

    def end(self, sems):
        self.nc.clear_and_free_semaphores(sems.all)
        self.nc.all_engine_barrier()

    def sbuf(self, ctx, name, shape, dt=F32):
        self.uid += 1
        return ctx.enter_context(self.nc.sbuf_tensor(f"{name}_{self.uid}", shape, dt))

    def const(self, name):
        a, n = self.const_at[name]
        return self.consts[:, a:a + n]


    def load(self, name, pairs):
        nc, sem = self.nc, self.Sems(self, name)
        loaded_sp, loaded_act = sem("loaded_sp"), sem("loaded_act")
        with nc.Block() as block:
            @block.sync
            def _(sp):
                for dst, src in pairs[0::2]:
                    sp.dma_start(dst, src).then_inc(loaded_sp, 16)
                sp.wait_ge(loaded_sp, 16 * len(pairs[0::2]))

            @block.scalar
            def _(act):
                for dst, src in pairs[1::2]:
                    act.dma_start(dst, src).then_inc(loaded_act, 16)
                if len(pairs) > 1:
                    act.wait_ge(loaded_act, 16 * len(pairs[1::2]))
        self.end(sem)

    def transpose(self, name, groups):
        nc, sem = self.nc, self.Sems(self, name)
        turned, out_v, out_a = sem("turned"), sem("out_v"), sem("out_a")
        banks = 8
        ident = self.const("ident")

        def psum_of(g):
            srcs, dst, _, _ = groups[g]
            w = srcs[0].shape[1]
            return self.ps[0:w, g % banks, 0:sum(s.shape[0] for s in srcs)]

        with nc.Block() as block:
            @block.tensor
            def _(pe):
                for g, (srcs, dst, _, _) in enumerate(groups):
                    if g >= banks:
                        pe.wait_ge(out_a if g % 2 else out_v, (g - banks) // 2 + 1)
                    at = 0
                    for s in srcs:
                        n = s.shape[0]
                        ins = pe.transpose(psum_of(g)[:, at:at + n], s, ident[0:n, 0:n])
                        at += n
                    ins.then_inc(turned, 1)

            @block.vector
            def _(dve):
                for g in range(0, len(groups), 2):
                    srcs, dst, scale, bias = groups[g]
                    dve.wait_ge(turned, g + 1)
                    if scale is None:
                        dve.tensor_copy(dst, psum_of(g)).then_inc(out_v, 1)
                    elif bias is None:
                        dve.tensor_scalar(dst, psum_of(g), scale, None, ALU.mult).then_inc(out_v, 1)
                    else:
                        dve.tensor_scalar(dst, psum_of(g), scale, bias, ALU.mult, ALU.add).then_inc(out_v, 1)

            @block.scalar
            def _(act):
                for g in range(1, len(groups), 2):
                    srcs, dst, scale, bias = groups[g]
                    act.wait_ge(turned, g + 1)
                    if scale is None:
                        act.copy(dst, psum_of(g)).then_inc(out_a, 1)
                    elif bias is None:
                        act.activation(dst, psum_of(g), ACT.Copy, scale=scale).then_inc(out_a, 1)
                    else:
                        act.activation(dst, psum_of(g), ACT.Identity, bias=bias, scale=scale).then_inc(out_a, 1)
        self.end(sem)

    def project(self, name, ring, slots):
        nc, sem = self.nc, self.Sems(self, name)
        R = ring.shape[1]
        w_in = [sem(f"weights{r}") for r in range(R)]
        product, out_v, out_a, step = sem("product"), sem("out_v"), sem("out_a"), sem("step")
        banks = 8
        jobs, last_of_slot = [], []
        for s, (_, js) in enumerate(slots):
            for j in js:
                jobs.append((s, *j))
            last_of_slot.append(len(jobs))
        for s in range(len(slots) - 2, -1, -1):
            if not slots[s][1]:
                last_of_slot[s] = last_of_slot[s + 1]
        leaves, count = [], [0, 0]
        for n, (s, out, pairs, leave) in enumerate(jobs):
            a = leave[0] == "copy" and n % 2
            leaves.append((a, count[a]))
            count[a] += 1
        tmp_ctx = ExitStack()
        tmp = self.sbuf(tmp_ctx, "gated", [P, BANK])

        def psum_of(n):
            out = jobs[n][1]
            return self.ps[0:out.shape[0], n % banks, 0:out.shape[1]]

        with nc.Block() as block:
            @block.sync
            def _(sp):
                for s, (src, _) in enumerate(slots):
                    if s >= R:
                        sp.wait_ge(product, last_of_slot[s - R])
                    sp.dma_start(ring[0:src.shape[0], s % R, 0:src.shape[1]], src).then_inc(w_in[s % R], 16)

            @block.tensor
            def _(pe):
                seen = -1
                for n, (s, out, pairs, leave) in enumerate(jobs):
                    while seen < s:
                        seen += 1
                        pe.wait_ge(w_in[seen % R], 16 * (seen // R + 1))
                    if n >= banks:
                        a, c = leaves[n - banks]
                        pe.wait_ge(out_a if a else out_v, c + 1)
                    for k, (lhs, rhs) in enumerate(pairs):
                        ins = pe.matmul(psum_of(n), lhs, rhs, start=(k == 0), stop=(k == len(pairs) - 1))
                    ins.then_inc(product, 1)

            @block.vector
            def _(dve):
                order = Order(dve, step)
                for n, (s, out, pairs, leave) in enumerate(jobs):
                    if leaves[n][0]:
                        continue
                    dve.wait_ge(product, n + 1)
                    if leave[0] == "copy":
                        if leave[1] is None:
                            dve.tensor_copy(out, psum_of(n)).then_inc(out_v, 1)
                        else:
                            dve.tensor_scalar(out, psum_of(n), leave[1], None, ALU.mult).then_inc(out_v, 1)
                    elif leave[0] == "residual":
                        dve.scalar_tensor_tensor(out=out, in0=out, scalar=leave[1], in1=psum_of(n),
                                                 op0=ALU.mult, op1=ALU.add).then_inc(out_v, 1)
                    elif leave[0] == "plus":
                        dve.tensor_tensor(out, psum_of(n), leave[1], ALU.add).then_inc(out_v, 1)
                    else:
                        order.done(dve.tensor_tensor(tmp[:, :], psum_of(n), leave[1], ALU.mult))
                        dve.tensor_tensor(out, out, tmp[:, :], ALU.add).then_inc(out_v, 1)
                        dve.wait_ge(out_v, leaves[n][1] + 1)

            @block.scalar
            def _(act):
                for n, (s, out, pairs, leave) in enumerate(jobs):
                    if not leaves[n][0]:
                        continue
                    act.wait_ge(product, n + 1)
                    if leave[1] is None:
                        act.copy(out, psum_of(n)).then_inc(out_a, 1)
                    else:
                        act.activation(out, psum_of(n), ACT.Copy, scale=leave[1]).then_inc(out_a, 1)
        tmp_ctx.close()
        self.end(sem)

    def split(self, name, parts):
        nc, sem = self.nc, self.Sems(self, name)
        high_done = sem("high_done")
        with nc.Block() as block:
            @block.scalar
            def _(act):
                for src, high, low in parts:
                    act.copy(high, src).then_inc(high_done, 1)

            @block.vector
            def _(dve):
                for n, (src, high, low) in enumerate(parts):
                    dve.wait_ge(high_done, n + 1)
                    dve.tensor_tensor(low, src, high.bitcast(F32), ALU.subtract)
        self.end(sem)

    def stream(self, name, X, K, blocks):
        nc, sem = self.nc, self.Sems(self, name)
        R, S, banks = 4, 2, 8
        ntok = X.shape[2]
        raw_in = [sem(f"raw_in{r}") for r in range(R)]
        high, low, used = sem("high"), sem("low"), sem("used")
        out_v, out_a, step = sem("out_v"), sem("out_a"), sem("step")
        ctx = ExitStack()
        W = self.sbuf(ctx, "w_raw", [P, R, BANK])
        WS = [self.sbuf(ctx, n, [P, S, BANK], F32R) for n in ("w_high", "w_low")]
        XS = [self.sbuf(ctx, n, [P, S, ntok], F32R) for n in ("x_high", "x_low")]
        tmp = self.sbuf(ctx, "gated", [P, BANK])
        x_tile = lambda k: X[:, bass.ds(k, 1), :].rearrange("p e n -> p (e n)")
        peeled = K if K < 8 else (K % 4 or 4)
        jobs = [(c, *j) for c, (_, _, _, js) in enumerate(blocks) for j in js]
        first_job = [sum(len(b[3]) for b in blocks[:c]) for c in range(len(blocks) + 1)]
        by_act = [j[4][0] == "copy" and g % 2 == 1 for g, j in enumerate(jobs)]
        turn = [sum(1 for h in range(g) if by_act[h] == by_act[g]) for g in range(len(jobs))]

        def psum_of(g):
            _, (a, b), (x, y), _, _ = jobs[g]
            return self.ps[0:b - a, g % banks, 0:y - x]

        def tiles(eng, tile, between=None):
            for c in range(len(blocks)):
                for k in range(K):
                    n = c * K + k
                    if k == peeled and K > peeled + 4:
                        with eng.Fori(0, (K - peeled - 4) // 4) as i:
                            for j in range(4):
                                tile(c, i * 4 + (peeled + j), i * 4 + (n + j), (n + j) % R, i + (n + j) // 4)
                    if k < peeled or k >= K - 4:
                        tile(c, k, n, n % R, n // R)
                    if between:
                        between(c, k)

        def leaves_between(leave, act):
            def between(c, k):
                if c and k < 2:
                    js = [g for g in range(first_job[c - 1], first_job[c]) if by_act[g] == act]
                    half = 1 if len(js) > 1 else len(js)
                    for g in (js[:half] if k == 0 else js[half:]):
                        leave(g)
            return between

        def leave_last(leave, act):
            for g in range(first_job[-2], first_job[-1]):
                if by_act[g] == act:
                    leave(g)

        with nc.Block() as block:
            @block.sync
            def _(sp):
                def tile(c, k, n, rest, turns):
                    src, w = blocks[c][0], blocks[c][1]
                    sp.wait_ge(low, n + 1)
                    sp.dma_start(W[:, rest, 0:w], src[:, bass.ds(k * w, w)]).then_inc(raw_in[rest], 16)
                tiles(sp, tile)

            @block.scalar
            def _(act):
                act.sem_inc(used, S)

                def tile(c, k, n, rest, turns):
                    w = blocks[c][1]
                    act.wait_ge(raw_in[rest], turns * 16 + 16)
                    act.wait_ge(used, n + 1)
                    act.copy(WS[0][:, rest % S, 0:w], W[:, rest, 0:w])
                    act.copy(XS[0][:, rest % S, :], x_tile(k)).then_inc(high, 1)

                def leave(g):
                    c, _, _, out, (kind, scale) = jobs[g]
                    act.wait_ge(used, (c + 1) * K + S)
                    if scale is None:
                        act.copy(out, psum_of(g)).then_inc(out_a, 1)
                    else:
                        act.activation(out, psum_of(g), ACT.Copy, scale=scale).then_inc(out_a, 1)

                tiles(act, tile, leaves_between(leave, True))
                leave_last(leave, True)

            @block.vector
            def _(dve):
                dve.sem_inc(low, R)
                order = Order(dve, step)

                def tile(c, k, n, rest, turns):
                    w = blocks[c][1]
                    dve.wait_ge(high, n + 1)
                    dve.tensor_tensor(XS[1][:, rest % S, :], x_tile(k),
                                      XS[0][:, rest % S, :].bitcast(F32), ALU.subtract)
                    dve.tensor_tensor(WS[1][:, rest % S, 0:w], W[:, rest, 0:w],
                                      WS[0][:, rest % S, 0:w].bitcast(F32), ALU.subtract).then_inc(low, 1)

                def leave(g):
                    c, _, _, out, (kind, arg) = jobs[g]
                    dve.wait_ge(used, (c + 1) * K + S)
                    if kind == "copy" and arg is None:
                        dve.tensor_copy(out, psum_of(g)).then_inc(out_v, 1)
                    elif kind == "copy":
                        dve.tensor_scalar(out, psum_of(g), arg, None, ALU.mult).then_inc(out_v, 1)
                    elif kind == "residual":
                        dve.scalar_tensor_tensor(out=out, in0=out, scalar=arg, in1=psum_of(g),
                                                 op0=ALU.mult, op1=ALU.add).then_inc(out_v, 1)
                    else:
                        order.done(dve.tensor_tensor(tmp[:, :], psum_of(g), arg, ALU.mult))
                        dve.tensor_tensor(out, out, tmp[:, :], ALU.add).then_inc(out_v, 1)
                        dve.wait_ge(out_v, turn[g] + 1)

                tiles(dve, tile, leaves_between(leave, False))
                leave_last(leave, False)

            @block.tensor
            def _(pe):
                def tile(c, k, n, rest, turns):
                    by_weights, js = blocks[c][2], range(first_job[c], first_job[c + 1])
                    pe.wait_ge(low, n + (1 + R))
                    start = isinstance(k, int) and k == 0
                    stop = isinstance(k, int) and k == K - 1
                    for g in js:
                        if start and g >= banks:
                            pe.wait_ge(out_a if by_act[g - banks] else out_v, turn[g - banks] + 1)
                        _, (a, b), (x, y), _, _ = jobs[g]
                        for first, second in ((0, 0), (0, 1), (1, 0)):
                            st, mv = (WS[first], XS[second]) if by_weights else (XS[first], WS[second])
                            ins_ = pe.matmul(psum_of(g), st[:, rest % S, a:b], mv[:, rest % S, x:y],
                                             start=start and first + second == 0, stop=stop and first == 1)
                    ins_.then_inc(used, 1)
                tiles(pe, tile)
        ctx.close()
        self.end(sem)

    def rows_block(self, src, n, tiles, out, leave):
        return (src, n, False, [((t * P, (t + 1) * P), (0, n), out(t), leave(t)) for t in range(tiles)])

    def attention(self, name, units, dk, dv=DH):
        nc, sem = self.nc, self.Sems(self, name)
        scored, exps, turned, turned_out, mixed, left = (sem(n) for n in (
            "scored", "exps", "turned", "turned_out", "mixed", "left"))
        shifted, masked, act_step, dve_step = sem("shifted"), sem("masked"), sem("act_step"), sem("dve_step")
        NK = max(sum(k.shape[1] for k in u[1]) for u in units)
        ctx = ExitStack()
        s_sb = self.sbuf(ctx, "scores", [P, 2, NK])
        e_sb = self.sbuf(ctx, "exps", [P, 2, NK])
        pT = self.sbuf(ctx, "expsT", [P, 2, NK])
        stat = self.sbuf(ctx, "stat", [P, 4, 8])
        ident = self.const("ident")
        U = len(units)
        LAG = 3
        nk = [sum(k.shape[1] for k in u[1]) for u in units]
        S = [self.ps[:, 0:2, :].rearrange("p b n -> p (b n)"), self.ps[:, 2:4, :].rearrange("p b n -> p (b n)")]
        TP = self.ps[:, 4:6, :].rearrange("p b n -> p (b n)")
        O = [self.ps[:, 6, 0:dv], self.ps[:, 7, 0:dv]]

        with nc.Block() as block:
            @block.tensor
            def _(pe):
                def scores(u):
                    if u >= 2:
                        pe.wait_ge(masked, u - 1)
                    at = 0
                    for k in units[u][1]:
                        n = k.shape[1]
                        ins = pe.matmul(S[u % 2][:, at:at + n], units[u][0], k, start=True, stop=True)
                        at += n
                    ins.then_inc(scored, 1)

                def turn(u):
                    pe.wait_ge(exps, u + 1)
                    if u >= 1:
                        pe.wait_ge(turned_out, u)
                    for c in range(nk[u] // P):
                        ins = pe.transpose(TP[:, c * P:(c + 1) * P], e_sb[:, u % 2, c * P:(c + 1) * P], ident)
                    ins.then_inc(turned, 1)

                def mix(u):
                    pe.wait_ge(turned_out, u + 1)
                    if u >= 2:
                        pe.wait_ge(left, u - 1)
                    n = nk[u] // P
                    for c in range(n):
                        ins = pe.matmul(O[u % 2], pT[:, u % 2, c * P:(c + 1) * P], units[u][4][c],
                                        start=(c == 0), stop=(c == n - 1))
                    ins.then_inc(mixed, 1)

                scores(0)
                if U > 1:
                    scores(1)
                for u in range(U):
                    turn(u)
                    if u + 2 < U:
                        scores(u + 2)
                    if u >= 1:
                        mix(u - 1)
                mix(U - 1)

            @block.vector
            def _(dve):
                order = Order(dve, dve_step)

                def leave(u):
                    b = u % 4
                    dve.wait_ge(exps, u + 1)
                    if units[u][3] is not None:
                        order.done(dve.tensor_tensor(stat[:, b, 4:5], stat[:, b, 2:3], stat[:, b, 3:4], ALU.add))
                        order.done(dve.reciprocal(stat[:, b, 5:6], stat[:, b, 4:5]))
                    else:
                        order.done(dve.reciprocal(stat[:, b, 5:6], stat[:, b, 2:3]))
                    dve.wait_ge(mixed, u + 1)
                    dve.tensor_scalar(units[u][5], O[u % 2], stat[:, b, 5:6], None, ALU.mult).then_inc(left, 1)

                for u in range(U):
                    b, n = u % 2, nk[u]
                    dve.wait_ge(scored, u + 1)
                    if u >= 2:
                        dve.wait_ge(exps, u - 1)
                    mask, at = units[u][2], 0
                    for piece in mask:
                        w = piece if isinstance(piece, int) else int(np.prod(piece.shape[1:]))
                        out_, in_ = s_sb[:, b, at:at + w], S[b][:, at:at + w]
                        if isinstance(piece, int):
                            ins = dve.tensor_copy(out_, in_)
                        else:
                            if len(piece.shape) == 3:
                                out_, in_ = (x.rearrange("p (j c) -> p j c", c=piece.shape[2]) for x in (out_, in_))
                            ins = dve.tensor_tensor(out_, in_, piece, ALU.add)
                        at += w
                        if at < n:
                            order.done(ins)
                        else:
                            ins.then_inc(masked, 1)
                    dve.wait_ge(masked, u + 1)
                    order.done(dve.tensor_reduce(stat[:, u % 4, 0:1], s_sb[:, b, 0:n], AX_X, ALU.max))
                    sink = units[u][3]
                    dve.tensor_scalar(stat[:, u % 4, 1:2], stat[:, u % 4, 0:1], sink if sink is not None else NEG, -1.0,
                                      ALU.max, ALU.mult).then_inc(shifted, 1)
                    if u >= LAG:
                        leave(u - LAG)
                for u in range(max(U - LAG, 0), U):
                    leave(u)

            @block.scalar
            def _(act):
                def exp(u):
                    b, n = u % 2, nk[u]
                    act.wait_ge(shifted, u + 1)
                    if u >= 2:
                        act.wait_ge(turned, u - 1)
                    if u >= 4:
                        act.wait_ge(left, u - 3)
                    c = u % 4
                    if units[u][3] is not None:
                        act.activation(stat[:, c, 3:4], units[u][3], ACT.Exp, bias=stat[:, c, 1:2]).then_inc(act_step, 1)
                        act.wait_ge(act_step, u + 1)
                    act.activation(e_sb[:, b, 0:n], s_sb[:, b, 0:n], ACT.Exp, bias=stat[:, c, 1:2],
                                   accum_out=stat[:, c, 2:3]).then_inc(exps, 1)

                exp(0)
                if U > 1:
                    exp(1)
                for u in range(U):
                    act.wait_ge(turned, u + 1)
                    if u >= 2:
                        act.wait_ge(mixed, u - 1)
                    act.copy(pT[:, u % 2, 0:nk[u]], TP[:, 0:nk[u]]).then_inc(turned_out, 1)
                    if u + 2 < U:
                        exp(u + 2)
        ctx.close()
        self.end(sem)

    def norm(self, name, tiles, kind, eps, loads=()):
        nc, sem = self.nc, self.Sems(self, name)
        stats, roots, scales, step, loaded = (sem(n) for n in ("stats", "roots", "scales", "step", "loaded"))
        normed, gained, biased = sem("normed"), sem("gained"), sem("biased")
        ctx = ExitStack()
        n = len(tiles)
        pieces = [[(c, min(c + 512, t[0].shape[1])) for c in range(0, t[0].shape[1], 512)] for t in tiles]
        bn = self.sbuf(ctx, "bn", [P, n, 12])
        mv = self.sbuf(ctx, "mv", [P, n, 4])
        inv = self.sbuf(ctx, "inv", [P, n, 2])
        eps_t = self.sbuf(ctx, "eps", [P, 1])
        gains, biases = tiles[0][2] is not None, tiles[0][3] is not None
        by_act = [gains or i % 2 == 1 for i in range(n)]
        with nc.Block() as block:
            if loads:
                @block.sync
                def _(sp):
                    for dst, src in loads:
                        sp.dma_start(dst, src).then_inc(loaded, 16)

            @block.vector
            def _(dve):
                order = Order(dve, step)
                order.done(dve.memset(eps_t[:, :], eps))
                for i, (src, dst, gain, bias) in enumerate(tiles):
                    for c, (a, b) in enumerate(pieces[i]):
                        ins_ = dve.bn_stats(bn[:, i, 6 * c:6 * c + 6], src[:, a:b])
                    order.done(ins_)
                for i in range(n):
                    ins_ = dve.bn_aggr(mv[:, i, 0:2], bn[:, i, 0:6 * len(pieces[i])])
                order.done(ins_)
                if kind == "rms":
                    order.done(dve.tensor_tensor(mv[:, :, 2], mv[:, :, 0], mv[:, :, 0], ALU.mult))
                    order.done(dve.tensor_tensor(mv[:, :, 2], mv[:, :, 2], mv[:, :, 1], ALU.add))
                else:
                    order.done(dve.tensor_copy(mv[:, :, 2], mv[:, :, 1]))
                dve.sem_inc(stats, 1)
                dve.wait_ge(roots, 1)
                order.done(dve.reciprocal(inv[:, :, 0], mv[:, :, 3]))
                if kind == "ln":
                    order.done(dve.scalar_tensor_tensor(out=inv[:, :, 1], in0=mv[:, :, 0], scalar=-1.0,
                                                        in1=inv[:, :, 0], op0=ALU.mult, op1=ALU.mult))
                dve.sem_inc(scales, 1)
                if loads:
                    dve.wait_ge(loaded, 16 * len(loads))
                for i, (src, dst, gain, bias) in enumerate(tiles):
                    if not by_act[i]:
                        dve.tensor_scalar(dst, src, inv[:, i, 0:1], None, ALU.mult)
                    if gains:
                        dve.wait_ge(normed, i + 1)
                        dve.tensor_tensor(dst, dst, gain, ALU.mult).then_inc(gained, 1)
                if biases:
                    dve.wait_ge(gained, n)
                    dve.tensor_tensor(dst, dst, bias, ALU.add)

            @block.scalar
            def _(act):
                act.wait_ge(stats, 1)
                act.activation(mv[:, :, 3], mv[:, :, 2], ACT.Sqrt, bias=eps_t[:, :]).then_inc(roots, 1)
                act.wait_ge(scales, 1)
                for i, (src, dst, gain, bias) in enumerate(tiles):
                    if not by_act[i]:
                        continue
                    if kind == "rms":
                        act.activation(dst, src, ACT.Copy, scale=inv[:, i, 0:1]).then_inc(normed, 1)
                    else:
                        act.activation(dst, src, ACT.Identity, bias=inv[:, i, 1:2],
                                       scale=inv[:, i, 0:1]).then_inc(normed, 1)

            @block.gpsimd
            def _(pool):
                if biases:
                    pool.wait_ge(loaded, 16 * len(loads))
                    for i, (src, dst, gain, bias) in enumerate(tiles[:-1]):
                        pool.wait_ge(gained, i + 1)
                        pool.tensor_tensor(dst, dst, bias, ALU.add).then_inc(biased, 1)
                    pool.wait_ge(biased, n - 1)
        ctx.close()
        self.end(sem)

    def rope_halves(self, name, jobs):
        nc, sem = self.nc, self.Sems(self, name)
        step = sem("step")
        with nc.Block() as block:
            @block.vector
            def _(dve):
                order = Order(dve, step)
                for x1, x2, cos, sin, t1, t2, t3 in jobs:
                    order.done(dve.tensor_tensor(t1, x2, sin, ALU.mult))
                    order.done(dve.tensor_tensor(t2, x1, sin, ALU.mult))
                    order.done(dve.tensor_tensor(t3, x1, cos, ALU.mult))
                    order.done(dve.tensor_tensor(x1, t3, t1, ALU.subtract))
                    order.done(dve.tensor_tensor(t3, x2, cos, ALU.mult))
                    order.done(dve.tensor_tensor(x2, t3, t2, ALU.add))
        self.end(sem)

    def layer_norm(self, name, i, j):
        with ExitStack() as ctx:
            g = self.sbuf(ctx, "gain", [P, DM])
            b = self.sbuf(ctx, "bias", [P, DM])
            row = lambda a: a[i, j:j + 1, :].broadcast_to([P, DM])
            self.norm(name, [(self.H[:, t, :], self.H[:, t, :], g[:, :], b[:, :]) for t in range(NT)], "ln", LN_EPS,
                      [(g[:, :], row(self.ins["ln_g"])), (b[:, :], row(self.ins["ln_b"]))])

    def transpose_rows(self, name, X, tiles, XT, scale=None, bias=None, at=0):
        groups = []
        for k in range(KD):
            for a in range(0, tiles, 4):
                b = min(a + 4, tiles)
                groups.append(([X[:, t, k * P:(k + 1) * P] for t in range(a, b)],
                               XT[:, k, at + a * P:at + b * P],
                               None if scale is None else scale[:, k:k + 1],
                               None if bias is None else bias[:, k:k + 1]))
        self.transpose(name, groups)


    def window_layer(self):
        ins, H = self.ins, self.H
        with ExitStack() as outer:
            O = self.sbuf(outer, "o_rows", [P, NT, DM])
            with ExitStack() as ctx:
                QKV = self.sbuf(ctx, "qkv", [P, NT, 3 * BANK])
                with ExitStack() as c2:
                    XT = self.sbuf(c2, "xT", [P, KD, T])
                    self.transpose_rows("a_xT", H, NT, XT)
                    self.stream("a_qkv", XT[:, :, :], KD, [
                        self.rows_block(ins["a_w_in"][c], BANK, NT,
                                        lambda t, c=c: QKV[:, t, c * BANK:(c + 1) * BANK],
                                        lambda t: ("copy", None)) for c in range(3)])
                nh = A_HEADS + A_KV
                with ExitStack() as c2:
                    tm = self.sbuf(c2, "rope_tmp", [P, 3, NT, nh, A_ROT])
                    x = QKV[:, :, 0:nh * DH].rearrange("p t (h d) -> p t h d", h=nh)
                    cos = self.const("rope_a_cos").rearrange("p (t d) -> p t d", t=NT)
                    sin = self.const("rope_a_sin").rearrange("p (t d) -> p t d", t=NT)
                    jobs = []
                    for t in range(NT):
                        bc = lambda a: a[:, t, :].unsqueeze(1).broadcast_to([P, nh, A_ROT])
                        jobs.append((x[:, t, :, 0:A_ROT], x[:, t, :, A_ROT:2 * A_ROT], bc(cos), bc(sin),
                                     tm[:, 0, t], tm[:, 1, t], tm[:, 2, t]))
                    self.rope_halves("a_rope", jobs)
                QT = self.sbuf(ctx, "qT", [P, A_HEADS // 2, T])
                KT = self.sbuf(ctx, "kT", [P, A_KV, T])
                K2 = self.sbuf(ctx, "k_twice", [P, NT, A_KV, 2, DH])
                groups = [([QKV[:, t, j * P:(j + 1) * P] for t in range(NT)], QT[:, j, :], DH ** -0.5, None)
                          for j in range(A_HEADS // 2)]
                self.transpose("a_qT", groups)
                sem = self.Sems(self, "a_k2")
                copied = sem("copied")
                with self.nc.Block() as block:
                    @block.vector
                    def _(dve):
                        for t in range(NT):
                            for half in range(2):
                                dve.tensor_copy(K2[:, t, :, half, :],
                                                QKV[:, t, A_HEADS * DH:(A_HEADS + A_KV) * DH].rearrange(
                                                    "p (h d) -> p h d", h=A_KV)).then_inc(copied, 1)
                        dve.wait_ge(copied, 2 * NT)
                self.end(sem)
                self.transpose("a_kT", [([K2[:, t, h].rearrange("p a d -> p (a d)") for t in range(NT)],
                                         KT[:, h, :], None, None) for h in range(A_KV)])
                units = []
                for t in range(NT):
                    for h in range(A_HEADS):
                        r = (h % 2) * DH
                        a = max(t - 1, 0)
                        mask = self.const("window")
                        kv = h // (A_HEADS // A_KV)
                        units.append((QT[r:r + DH, h // 2, t * P:(t + 1) * P],
                                      [KT[r:r + DH, kv, a * P:(t + 1) * P]],
                                      [mask[:, 0:2 * P] if t else mask[:, P:2 * P]],
                                      self.sinks[:, h:h + 1],
                                      [QKV[:, c, (A_HEADS + A_KV + kv) * DH:(A_HEADS + A_KV + kv + 1) * DH]
                                       for c in range(a, t + 1)],
                                      O[:, t, h * DH:(h + 1) * DH]))
                self.attention("a_attn", units, DH)
            self.out_projection("a_out", O, ins["a_w_o"])
        self.layer_norm("a_ln", 0, 0)

    def out_projection(self, name, O, w_dram):
        with ExitStack() as ctx:
            OT = self.sbuf(ctx, "oT", [P, KD, T])
            self.transpose_rows(name + "_T", O, NT, OT)
            self.stream(name, OT[:, :, :], KD, [
                self.rows_block(w_dram[c], BANK, NT, lambda t, c=c: self.H[:, t, c * BANK:(c + 1) * BANK],
                                lambda t: ("residual", ALPHA)) for c in range(2)])


    def route(self, layer, cm):
        nc, ins, H = self.nc, self.ins, self.H
        table = self.table[layer]
        n_log = GROUPS + EXPERTS
        with ExitStack() as ctx:
            LG = self.sbuf(ctx, "logits", [P, NT, n_log])
            with ExitStack() as c2:
                HT = self.sbuf(c2, "hT", [P, KD, T])
                ring = self.sbuf(c2, "ring", [P, 1, KD * n_log])
                self.transpose_rows(f"r{layer}_T", H, NT, HT)
                w = ring[:, 0, :].rearrange("p (k n) -> p k n", k=KD)
                self.project(f"r{layer}_logits", ring, [(ins["router"][layer], [
                    (LG[:, t, :], [(HT[:, k, t * P:(t + 1) * P], w[:, k, :]) for k in range(KD)],
                     ("copy", None)) for t in range(NT)])])

            sem = self.Sems(self, f"r{layer}")
            (rows_out, filled, table_filled, grouped, ranked, picked, counted, addressed, scattered, listed, exp_g,
             exp_2, step) = (sem(n) for n in (
                "rows_out", "filled", "table_filled", "grouped", "ranked", "picked", "counted", "addressed",
                "scattered", "listed", "exp_g", "exp_2", "step"))
            sb = lambda n, s, dt=F32: self.sbuf(ctx, n, s, dt)
            sentinel = sb("sentinel", [P, P], I32)
            gmax, gsum, gw, gd, ge = sb("gmax", [P, NT]), sb("gsum", [P, NT]), sb("gw", [P, NT]), \
                sb("gd", [P, NT, GROUPS]), sb("ge", [P, NT, GROUPS])
            eq, cand, first = sb("eq", [P, NT, EXPERTS]), sb("cand", [P, NT, EXPERTS]), sb("first", [P, NT])
            goh, outside = sb("goh", [P, NT, GROUPS]), sb("outside", [P, NT, GROUPS])
            EL = [sb(f"el{r}", [P, NT, EXPERTS]) for r in range(2)]
            OH = [sb(f"oh{r}", [P, NT, EXPERTS]) for r in range(2)]
            M = [sb(f"max{r}", [P, NT]) for r in range(2)]
            both = sb("both", [P, NT, EXPERTS])
            d21, e21, den = sb("d21", [P, NT]), sb("e21", [P, NT]), sb("den", [P, NT])
            pos, prod = sb("pos", [P, NT, EXPERTS]), sb("prod", [P, NT, EXPERTS])
            place, expert = sb("place", [P, NT, 2]), sb("expert", [P, NT, 2])
            address = sb("address", [P, NT * 2], I32)
            number = sb("number", [P, NT * 2], I32)
            most, over, passes = sb("most", [P, 1]), sb("over", [P, 3]), sb("passes", [P, 1])
            iota = self.const("experts")
            ones, before = self.const("ones"), self.const("before")
            POS = self.ps[:, 0, 0:NT * EXPERTS].rearrange("p (t e) -> p t e", t=NT)
            CNT = self.ps[:, 1, 0:EXPERTS]
            bc = lambda a, n: a.unsqueeze(2).broadcast_to([P, NT, n])
            io = lambda n: iota[:, 0:n].unsqueeze(1).broadcast_to([P, NT, n])

            with nc.Block() as block:
                @block.sync
                def _(sp):
                    sp.dma_start(self.rows.rearrange("(t p) d -> p t d", p=P), H[:, :, :]).then_inc(rows_out, 16)
                    sp.wait_ge(filled, 1)
                    sp.dma_start(table.rearrange("(p n) o -> p (n o)", p=P), sentinel[:, :]).then_inc(table_filled, 16)
                    sp.wait_ge(scattered, 16 * NT * 2)
                    sp.dma_start(cm["slots"][:, :, :],
                                 table.rearrange("(t p e) o -> p t (e o)", t=NT, p=P)).then_inc(listed, 16)
                    sp.wait_ge(rows_out, 16)
                    sp.wait_ge(listed, 16)

                @block.gpsimd
                def _(pool):
                    pool.memset(sentinel[:, :], SENTINEL).then_inc(filled, 1)
                    pool.wait_ge(table_filled, 16)
                    pool.wait_ge(addressed, 2)
                    for n in range(NT * 2):
                        pool.indirect_dma_start(out=table, out_offset=bass.IndirectOffsetOnAxis(
                            ap=address[:, n:n + 1], axis=0), in_=number[:, n:n + 1], in_offset=None,
                            bounds_check=EXPERTS * T - 1, oob_is_err=False).then_inc(scattered, 16)
                    pool.wait_ge(scattered, 16 * NT * 2)

                @block.vector
                def _(dve):
                    order = Order(dve, step)

                    def first_of(logits, n, largest, onehot):
                        e, c = eq[:, :, 0:n], cand[:, :, 0:n]
                        order.done(dve.tensor_reduce(largest, logits, AX_X, ALU.max))
                        order.done(dve.tensor_tensor(e, logits, bc(largest, n), ALU.is_equal))
                        order.done(dve.scalar_tensor_tensor(out=c, in0=e, scalar=-64.0, in1=io(n),
                                                            op0=ALU.mult, op1=ALU.add))
                        order.done(dve.tensor_reduce(first[:, :], c, AX_X, ALU.min))
                        order.done(dve.scalar_tensor_tensor(out=onehot, in0=io(n), scalar=-64.0,
                                                            in1=bc(first[:, :], n), op0=ALU.add, op1=ALU.is_equal))

                    lg = LG[:, :, 0:GROUPS]
                    first_of(lg, GROUPS, gmax[:, :], goh[:, :, :])
                    order.done(dve.tensor_tensor(gd[:, :, :], lg, bc(gmax[:, :], GROUPS), ALU.subtract))
                    dve.sem_inc(grouped, 1)
                    order.done(dve.tensor_scalar(outside[:, :, :], goh[:, :, :], -1.0, -NEG, ALU.add, ALU.mult))
                    for t in range(NT):
                        order.done(dve.tensor_tensor(
                            EL[0][:, t, :].rearrange("p (g e) -> p g e", g=GROUPS),
                            LG[:, t, GROUPS:].rearrange("p (g e) -> p g e", g=GROUPS),
                            outside[:, t, :].unsqueeze(2).broadcast_to([P, GROUPS, PER_GROUP]), ALU.add))
                    first_of(EL[0][:, :, :], EXPERTS, M[0][:, :], OH[0][:, :, :])
                    order.done(dve.scalar_tensor_tensor(out=EL[1][:, :, :], in0=OH[0][:, :, :], scalar=NEG,
                                                        in1=EL[0][:, :, :], op0=ALU.mult, op1=ALU.add))
                    first_of(EL[1][:, :, :], EXPERTS, M[1][:, :], OH[1][:, :, :])
                    order.done(dve.tensor_tensor(d21[:, :], M[1][:, :], M[0][:, :], ALU.subtract))
                    dve.sem_inc(ranked, 1)
                    order.done(dve.tensor_tensor(both[:, :, :], OH[0][:, :, :], OH[1][:, :, :], ALU.add))
                    dve.sem_inc(picked, 1)
                    dve.wait_ge(exp_g, 1)
                    order.done(dve.tensor_reduce(gsum[:, :], ge[:, :, :], AX_X, ALU.add))
                    order.done(dve.reciprocal(gw[:, :], gsum[:, :]))
                    dve.wait_ge(exp_2, 1)
                    order.done(dve.tensor_scalar(den[:, :], e21[:, :], 1.0, None, ALU.add))
                    order.done(dve.reciprocal(first[:, :], den[:, :]))
                    order.done(dve.tensor_tensor(cm["weight"][:, :, 0], gw[:, :], first[:, :], ALU.mult))
                    order.done(dve.tensor_tensor(cm["weight"][:, :, 1], cm["weight"][:, :, 0], e21[:, :], ALU.mult))
                    dve.wait_ge(counted, 1)
                    order.done(dve.tensor_copy(pos[:, :, :], POS))
                    for r in range(2):
                        order.done(dve.tensor_tensor(prod[:, :, :], OH[r][:, :, :], pos[:, :, :], ALU.mult))
                        order.done(dve.tensor_reduce(place[:, :, r], prod[:, :, :], AX_X, ALU.add))
                        order.done(dve.tensor_tensor(prod[:, :, :], OH[r][:, :, :], io(EXPERTS), ALU.mult))
                        order.done(dve.tensor_reduce(expert[:, :, r], prod[:, :, :], AX_X, ALU.add))
                    dve.scalar_tensor_tensor(out=address[:, :].rearrange("p (t r) -> p t r", r=2), in0=place[:, :, :],
                                             scalar=float(EXPERTS), in1=expert[:, :, :],
                                             op0=ALU.mult, op1=ALU.add).then_inc(addressed, 1)
                    dve.tensor_copy(number[:, :], self.const("assignment")).then_inc(addressed, 1)
                    order.done(dve.tensor_reduce(most[:, :], CNT, AX_X, ALU.max))
                    for c in range(3):
                        order.done(dve.tensor_scalar(over[:, c:c + 1], most[:, :], float(P * (c + 1)), None, ALU.is_gt))
                    order.done(dve.tensor_reduce(passes[:, :], over[:, :], AX_X, ALU.add))
                    order.done(dve.tensor_scalar(cm["passes"][:, :], passes[:, :], 1.0, None, ALU.add))
                    dve.wait_ge(listed, 16)
                    order.done(dve.tensor_scalar(cm["tokens"][:, :, :], cm["slots"][:, :, :], 1, None,
                                                 ALU.logical_shift_right))

                @block.scalar
                def _(act):
                    act.wait_ge(grouped, 1)
                    act.activation(ge[:, :, :], gd[:, :, :], ACT.Exp).then_inc(exp_g, 1)
                    act.wait_ge(ranked, 1)
                    act.activation(e21[:, :], d21[:, :], ACT.Exp).then_inc(exp_2, 1)

                @block.tensor
                def _(pe):
                    pe.wait_ge(picked, 1)
                    for t in range(NT):
                        for e in range(t):
                            pe.matmul(POS[:, t, :], ones, both[:, e, :], start=(e == 0), stop=False)
                        pe.matmul(POS[:, t, :], before, both[:, t, :], start=(t == 0), stop=True)
                    for t in range(NT):
                        ins_ = pe.matmul(CNT, ones, both[:, t, :], start=(t == 0), stop=(t == NT - 1))
                    ins_.then_inc(counted, 1)
            self.end(sem)

    def experts(self, layer, cm):
        nc, ins = self.nc, self.ins
        weights = [ins[f"moe_{n}"] for n in ("gate", "up", "down")]
        base = layer * EXPERTS
        Y = self.Y[layer]
        HALF = EXPERTS // 2
        UNIT = KD * HID // 2
        ORDER = [(0, 0, 0), (0, 0, 1), (1, 0, 0), (1, 0, 1), (0, 1, 0), (0, 1, 1),
                 (1, 1, 0), (1, 1, 1), (2, 0, 0), (2, 0, 1), (2, 1, 0), (2, 1, 1)]
        NU = len(ORDER)
        RAW, SPLIT = 6, 4
        with ExitStack() as ctx:
            sem = self.Sems(self, f"e{layer}")
            raw_in = [sem(f"raw_in{r}") for r in range(RAW)]
            gathered, scattered = ([sem(f"{n}{b}") for b in range(2)] for n in ("gathered", "scattered"))
            high, low, used = sem("high"), sem("low"), sem("used")
            x_turned, x_high, x_low = sem("x_turned"), sem("x_high"), sem("x_low")
            silu_done, hid_done, h_turned, h_high, h_low, y_out = (sem(n) for n in (
                "silu_done", "hid_done", "h_turned", "h_high", "h_low", "y_out"))
            stored = sem("stored")
            listed, cleared, free_to_move, blank = sem("listed"), sem("cleared"), sem("free_to_move"), sem("blank")
            sb = lambda n, s, dt=F32: self.sbuf(ctx, n, s, dt)
            WR = sb("w_raw", [P, RAW, UNIT])
            WS = [sb("w_high", [P, SPLIT, UNIT], F32R), sb("w_low", [P, SPLIT, UNIT], F32R)]
            XG = sb("xg", [P, 2, DM])
            XS = [sb("x_high", [P, 2, DM], F32R), sb("x_low", [P, 2, DM], F32R)]
            SG, HD = sb("sg", [P, 2, HID]), sb("hid", [P, 2, HID])
            HS = [sb("h_high", [P, 2, HID], F32R), sb("h_low", [P, 2, HID], F32R)]
            YS = sb("ys", [P, 2, DM])
            gidx, sidx = sb("gidx", [P, 2], I32), sb("sidx", [P, 2], I32)
            tokens = cm["tokens"][:, :, :].rearrange("p t e -> p (t e)")
            slots = cm["slots"][:, :, :].rearrange("p t e -> p (t e)")
            ident = self.const("ident")
            flat = lambda a: a.rearrange("p b n -> p (b n)")
            XB = YB = [self.ps[:, 0:2, :], self.ps[:, 2:4, :]]
            GB, UB, HB = self.ps[:, 4, :], self.ps[:, 5, :], self.ps[:, 6, :]

            def passes_of(eng):
                return eng.value_load(cm["passes"][0:1, 0:1], min_val=1, max_val=T // P)

            with nc.Block() as block:
                @block.sync
                def _(sp):
                    with sp.Fori(0, passes_of(sp)) as t, sp.Fori(0, HALF) as i:
                        n = t * HALF + i
                        for v, (m, b, half) in enumerate(ORDER):
                            sp.wait_ge(low, n * NU + v + 1)
                            sp.dma_start(WR[:, v % RAW, :], weights[m][bass.ds(i * 2 + (base + b), 1)].rearrange(
                                "e p n -> p (e n)")[:, half * UNIT:(half + 1) * UNIT]).then_inc(raw_in[v % RAW], 16)

                @block.gpsimd
                def _(pool):
                    pool.memset(XG[:, :, :], 0.0).then_inc(cleared, 1)
                    pool.memset(sidx[:, :], SENTINEL).then_inc(cleared, 1)
                    pool.wait_ge(cleared, 2)
                    pool.sem_inc(stored, 1)
                    passes = passes_of(pool)
                    last_token, last_assignment = pool.to_reg(T - 1), pool.to_reg(2 * T - 1)

                    def scatter(b):
                        pool.indirect_dma_start(out=Y, out_offset=bass.IndirectOffsetOnAxis(
                            ap=sidx[:, b:b + 1], axis=0), in_=YS[:, b, :], in_offset=None,
                            bounds_check=last_assignment, oob_is_err=False).then_inc(scattered[b], 16)

                    with pool.Fori(0, passes) as t, pool.Fori(0, HALF) as i:
                        n = t * HALF + i
                        for b in range(2):
                            pool.tensor_copy(gidx[:, b:b + 1], tokens[:, bass.ds(n * 2 + b, 1)]).then_inc(listed, 1)
                            pool.wait_ge(listed, n * 4 + b + 1)
                            pool.wait_ge(x_turned, n * 2 + b + 1)
                            pool.sem_inc(free_to_move, 1)
                            pool.indirect_dma_start(out=XG[:, b, :], out_offset=None, in_=self.rows,
                                                    in_offset=bass.IndirectOffsetOnAxis(ap=gidx[:, b:b + 1], axis=0),
                                                    bounds_check=last_token, oob_is_err=False).then_inc(gathered[b], 16)
                        for b in range(2):
                            pool.wait_ge(y_out, n * 2 + b + 1)
                            pool.sem_inc(free_to_move, 1)
                            scatter(b)
                        for b in range(2):
                            pool.wait_ge(scattered[b], n * 16 + 16)
                            pool.wait_ge(gathered[b], n * 16 + 16)
                            pool.tensor_copy(sidx[:, b:b + 1], slots[:, bass.ds(n * 2 + b, 1)]).then_inc(listed, 1)
                        if b == 1:
                            pool.sem_inc(stored, 1)
                    pool.wait_ge(listed, passes * (4 * HALF))
                    for b in range(2):
                        pool.wait_ge(y_out, passes * EXPERTS + b + 1)
                        pool.sem_inc(free_to_move, 1)
                        scatter(b)
                    for b in range(2):
                        pool.wait_ge(scattered[b], passes * (16 * HALF) + 16)

                @block.tensor
                def _(pe):
                    pe.sem_inc(used, SPLIT)
                    pe.sem_inc(x_turned, 2)
                    with pe.Fori(0, passes_of(pe)) as t, pe.Fori(0, HALF) as i:
                        n = t * HALF + i

                        def turn_x(b):
                            pe.wait_ge(gathered[b], n * 16 + 16)
                            pe.wait_ge(y_out, n * 2 + b + 1)
                            for k in range(KD):
                                ins_ = pe.transpose(XB[b][:, k // 4, (k % 4) * P:(k % 4 + 1) * P],
                                                    XG[:, b, k * P:(k + 1) * P], ident)
                            ins_.then_inc(x_turned, 1)

                        def unit(v):
                            m, b, half = ORDER[v]
                            s = v % SPLIT
                            pe.wait_ge(low, n * NU + v + 1 + RAW)
                            if m < 2:
                                out, tiles, per = (GB, UB)[m], KD, 1
                            else:
                                out, tiles, per = YB[b], HID // P, 2
                            if m == 0 and half == 0:
                                pe.wait_ge(x_low, n * 2 + b + 1)
                                pe.wait_ge(silu_done, n * 2 + b + 1)
                            if m == 1 and half == 0:
                                pe.wait_ge(hid_done, n * 2 + b + 1)
                            if m == 2 and half == 0:
                                pe.wait_ge(h_low, n * 2 + b + 2)
                            X = XS if m < 2 else HS
                            for k in range(tiles // 2):
                                kk = half * (tiles // 2) + k
                                for x, w in ((0, 0), (0, 1), (1, 0)):
                                    for c in range(per):
                                        ins_ = pe.matmul(
                                            out if per == 1 else out[:, c, :], X[x][:, b, kk * P:(kk + 1) * P],
                                            WS[w][:, s, (k * per + c) * BANK:(k * per + c + 1) * BANK],
                                            start=(kk == 0 and x + w == 0), stop=(kk == tiles - 1 and x == 1))
                            ins_.then_inc(used, 1)

                        def turn_h(b):
                            pe.wait_ge(hid_done, n * 2 + b + 2)
                            pe.wait_ge(h_low, n * 2 + b + 1)
                            for k in range(HID // P):
                                ins_ = pe.transpose(HB[:, k * P:(k + 1) * P], HD[:, b, k * P:(k + 1) * P], ident)
                            ins_.then_inc(h_turned, 1)

                        turn_x(0)
                        unit(0)
                        unit(1)
                        turn_x(1)
                        for v in range(2, 6):
                            unit(v)
                        turn_h(0)
                        for v in range(6, 10):
                            unit(v)
                        turn_h(1)
                        for v in range(10, 12):
                            unit(v)

                done = lambda n, v: n * NU + v + 1 + SPLIT

                @block.vector
                def _(dve):
                    dve.memset(self.ps[:, 0:4, :], 0.0).then_inc(blank, 1)
                    dve.sem_inc(low, RAW)
                    dve.sem_inc(hid_done, 1)
                    dve.sem_inc(h_low, 1)
                    with dve.Fori(0, passes_of(dve)) as t, dve.Fori(0, HALF) as i:
                        n = t * HALF + i

                        def lower(v):
                            dve.wait_ge(high, n * NU + v + 1)
                            dve.tensor_tensor(WS[1][:, v % SPLIT, :], WR[:, v % RAW, :],
                                              WS[0][:, v % SPLIT, :].bitcast(F32), ALU.subtract).then_inc(low, 1)

                        def lower_x(b):
                            dve.wait_ge(x_high, n * 2 + b + 1)
                            dve.tensor_tensor(XS[1][:, b, :], flat(XB[b]), XS[0][:, b, :].bitcast(F32),
                                              ALU.subtract).then_inc(x_low, 1)

                        def hidden(b):
                            dve.wait_ge(silu_done, n * 2 + b + 2)
                            dve.wait_ge(used, done(n, 3 if b == 0 else 7))
                            dve.tensor_tensor(HD[:, b, :], SG[:, b, :], UB, ALU.mult).then_inc(hid_done, 1)

                        def lower_h(b):
                            dve.wait_ge(h_high, n * 2 + b + 1)
                            dve.tensor_tensor(HS[1][:, b, :], HB, HS[0][:, b, :].bitcast(F32),
                                              ALU.subtract).then_inc(h_low, 1)

                        lower(0)
                        lower(1)
                        lower_x(0)
                        lower(2)
                        lower(3)
                        lower_x(1)
                        for v in range(4, 8):
                            lower(v)
                        hidden(0)
                        lower(8)
                        lower(9)
                        lower_h(0)
                        lower(10)
                        hidden(1)
                        lower(11)
                        lower_h(1)

                @block.scalar
                def _(act):
                    act.sem_inc(silu_done, 1)
                    act.wait_ge(blank, 1)

                    def y_copy(n, b):
                        act.wait_ge(used, done(n, 9 if b == 0 else 11) - NU)
                        act.wait_ge(stored, n + 1)
                        act.copy(YS[:, b, :], flat(YB[b])).then_inc(y_out, 1)

                    passes = passes_of(act)
                    with act.Fori(0, passes) as t, act.Fori(0, HALF) as i:
                        n = t * HALF + i

                        def raise_(v):
                            act.wait_ge(raw_in[v % RAW], n * 32 + 16 * (v // RAW) + 16)
                            act.wait_ge(used, n * NU + v + 1)
                            act.copy(WS[0][:, v % SPLIT, :], WR[:, v % RAW, :]).then_inc(high, 1)

                        def raise_x(b):
                            act.wait_ge(x_turned, n * 2 + b + 3)
                            act.copy(XS[0][:, b, :], flat(XB[b])).then_inc(x_high, 1)

                        def silu(b):
                            act.wait_ge(used, done(n, 1 if b == 0 else 5))
                            act.activation(SG[:, b, :], GB, ACT.Silu).then_inc(silu_done, 1)

                        def raise_h(b):
                            act.wait_ge(h_turned, n * 2 + b + 1)
                            act.copy(HS[0][:, b, :], HB).then_inc(h_high, 1)

                        raise_(0)
                        y_copy(n, 0)
                        raise_(1)
                        raise_x(0)
                        y_copy(n, 1)
                        raise_(2)
                        raise_(3)
                        raise_x(1)
                        raise_(4)
                        raise_(5)
                        silu(0)
                        for v in range(6, 10):
                            raise_(v)
                        silu(1)
                        raise_h(0)
                        raise_(10)
                        raise_(11)
                        raise_h(1)
                    y_copy(passes * HALF, 0)
                    y_copy(passes * HALF, 1)
            self.end(sem)

    def combine(self, layer, cm):
        nc, H = self.nc, self.H
        Y = self.Y[layer]
        with ExitStack() as ctx:
            sem = self.Sems(self, f"c{layer}")
            in_sp, step = [sem(f"in{t}") for t in range(NT)], sem("step")
            YT = self.sbuf(ctx, "y", [P, NT, 2, DM])
            with nc.Block() as block:
                @block.sync
                def _(sp):
                    for t in range(NT):
                        sp.dma_start(YT[:, t], Y[t * 2 * P:(t + 1) * 2 * P].rearrange("(p r) d -> p r d", r=2)).then_inc(in_sp[t], 16)
                @block.vector
                def _(dve):
                    order = Order(dve, step)
                    for t in range(NT):
                        order.done(dve.tensor_scalar(H[:, t, :], H[:, t, :], ALPHA, None, ALU.mult))
                        dve.wait_ge(in_sp[t], 16)
                        for r in range(2):
                            order.done(dve.scalar_tensor_tensor(out=H[:, t, :], in0=YT[:, t, r, :],
                                       scalar=cm["weight"][:, t, r:r + 1], in1=H[:, t, :], op0=ALU.mult, op1=ALU.add))
            self.end(sem)

    def moe_layer(self, layer):
        with ExitStack() as ctx:
            cm = {"weight": self.sbuf(ctx, "weight", [P, NT, 2]),
                  "passes": self.sbuf(ctx, "passes", [P, 1], I32),
                  "slots": self.sbuf(ctx, "slots", [P, NT, EXPERTS], I32),
                  "tokens": self.sbuf(ctx, "tokens", [P, NT, EXPERTS], I32)}
            self.route(layer, cm)
            self.experts(layer, cm)
            self.combine(layer, cm)
        self.layer_norm(f"m{layer}_ln", layer, 1)


    def latent_layer(self):
        ins, H, nc = self.ins, self.H, self.nc
        with ExitStack() as outer:
            O = self.sbuf(outer, "o_rows", [P, NT, DM])
            with ExitStack() as ctx:
                KV = self.sbuf(ctx, "kv", [P, NT, B_HEADS * (B_NOPE + B_V)])
                QT = self.sbuf(ctx, "qT", [B_DQ, B_HEADS, T])
                KR = self.sbuf(ctx, "k_rope", [P, NT, B_ROPE])
                with ExitStack() as c2:
                    C = self.sbuf(c2, "down", [P, NT, B_DOWN])
                    split = B_QR
                    gq, gkv = self.sbuf(c2, "gq", [P, B_QR]), self.sbuf(c2, "gkv", [P, B_KVR])
                    with ExitStack() as c3:
                        XT = self.sbuf(c3, "xT", [P, KD, T])
                        self.transpose_rows("b_xT", H, NT, XT)
                        self.stream("b_down", XT[:, :, :], KD, [
                            self.rows_block(src, n, NT, lambda t, a=a, n=n: C[:, t, a:a + n], lambda t: ("copy", None))
                            for src, a, n in ((ins["b_w_down_q"], 0, split),
                                              (ins["b_w_down_kv"], split, B_DOWN - split))])
                    self.norm("b_norms", [(C[:, t, a:b], C[:, t, a:b], g[:, :], None) for t in range(NT)
                                          for a, b, g in ((0, B_QR, gq), (B_QR, B_QR + B_KVR, gkv))],
                              "rms", RMS_EPS, [(gq[:, :], ins["b_q_norm"].broadcast_to([P, B_QR])),
                                               (gkv[:, :], ins["b_kv_norm"].broadcast_to([P, B_KVR]))])
                    half = B_ROPE // 2
                    cos = self.const("rope_b_cos").rearrange("p (t d) -> p t d", t=NT)
                    sin = self.const("rope_b_sin").rearrange("p (t d) -> p t d", t=NT)
                    with ExitStack() as c3:
                        tm = self.sbuf(c3, "rope_tmp", [P, 3, NT, half])
                        kr = C[:, :, B_QR + B_KVR:]
                        self.rope_halves("b_rope_k", [(kr[:, :, 0:half], kr[:, :, half:], cos, sin,
                                                       tm[:, 0], tm[:, 1], tm[:, 2])])
                    self.copies("b_kr", [(KR[:, :, :], C[:, :, B_QR + B_KVR:])])
                    NC = (B_QR + B_KVR) // P
                    CT = self.sbuf(c2, "downT", [P, NC, T])
                    self.transpose("b_cT", [([C[:, t, k * P:(k + 1) * P] for t in range(NT)], CT[:, k, :], None, None)
                                            for k in range(NC)])
                    Q = self.sbuf(c2, "q", [P, NT, B_HEADS * B_DQ])
                    kq, kkv = B_QR // P, B_KVR // P
                    self.stream("b_up_q", CT[:, 0:kq, :], kq, [
                        self.rows_block(ins["b_w_uq"][c], BANK, NT, lambda t, c=c: Q[:, t, c * BANK:(c + 1) * BANK],
                                        lambda t: ("copy", B_DQ ** -0.5)) for c in range(B_HEADS * B_DQ // BANK)])
                    self.stream("b_up_kv", CT[:, kq:, :], kkv, [
                        self.rows_block(ins["b_w_ukv"][c], BANK, NT, lambda t, c=c: KV[:, t, c * BANK:(c + 1) * BANK],
                                        lambda t: ("copy", None)) for c in range(B_HEADS * (B_NOPE + B_V) // BANK)])
                    with ExitStack() as c3:
                        tm = self.sbuf(c3, "rope_tmp", [P, 3, B_HEADS, half])
                        jobs = []
                        for t in range(NT):
                            x = Q[:, t, :].rearrange("p (h d) -> p h d", h=B_HEADS)
                            bc = lambda a: a[:, t, :].unsqueeze(1).broadcast_to([P, B_HEADS, half])
                            jobs.append((x[:, :, B_NOPE:B_NOPE + half], x[:, :, B_NOPE + half:], bc(cos), bc(sin),
                                         tm[:, 0], tm[:, 1], tm[:, 2]))
                        self.rope_halves("b_rope_q", jobs)
                    self.transpose("b_qT", [([Q[:, t, h * B_DQ:(h + 1) * B_DQ] for t in range(NT)],
                                             QT[:, h, :], None, None) for h in range(B_HEADS)])
                KT = self.sbuf(ctx, "kT", [B_DQ, B_HEADS, T])
                with ExitStack() as c2:
                    K = self.sbuf(c2, "k", [P, NT, B_HEADS, B_DQ])
                    pairs = []
                    for t in range(NT):
                        pairs.append((K[:, t, :, 0:B_NOPE],
                                      KV[:, t, :].rearrange("p (h d) -> p h d", h=B_HEADS)[:, :, 0:B_NOPE]))
                        pairs.append((K[:, t, :, B_NOPE:], KR[:, t, :].unsqueeze(1).broadcast_to([P, B_HEADS, B_ROPE])))
                    self.copies("b_k", pairs)
                    self.transpose("b_kT", [([K[:, t, h, :] for t in range(NT)], KT[:, h, :], None, None)
                                            for h in range(B_HEADS)])
                causal = self.const("causal")
                units = []
                for t in range(NT):
                    for h in range(B_HEADS):
                        v = h * (B_NOPE + B_V) + B_NOPE
                        units.append((QT[:, h, t * P:(t + 1) * P], [KT[:, h, 0:(t + 1) * P]],
                                      [causal[:, (NT - 1 - t) * P:T]], None,
                                      [KV[:, c, v:v + B_V] for c in range(t + 1)],
                                      O[:, t, h * B_V:(h + 1) * B_V]))
                self.attention("b_attn", units, B_DQ)
            self.out_projection("b_out", O, ins["b_w_o"])
        self.layer_norm("b_ln", 1, 0)

    def copies(self, name, pairs):
        nc, sem = self.nc, self.Sems(self, name)
        by_v, by_p = sem("by_v"), sem("by_p")
        with nc.Block() as block:
            @block.vector
            def _(dve):
                for dst, src in pairs[0::2]:
                    dve.tensor_copy(dst, src).then_inc(by_v, 1)
                dve.wait_ge(by_v, len(pairs[0::2]))

            @block.gpsimd
            def _(pool):
                for dst, src in pairs[1::2]:
                    pool.tensor_copy(dst, src).then_inc(by_p, 1)
                if len(pairs) > 1:
                    pool.wait_ge(by_p, len(pairs[1::2]))
        self.end(sem)


    def modulation(self):
        nc, ins = self.nc, self.ins
        NM = 6 * DM
        with ExitStack() as ctx:
            CR = self.sbuf(ctx, "c_columns", [P, KD, 2])
            CP = self.sbuf(ctx, "c_padded", [P, KD, P])
            CS = [self.sbuf(ctx, n, [P, KD, P], F32R) for n in ("c_high", "c_low")]
            rows = self.sbuf(ctx, "mod_rows", [2, DEPTH, NM])
            back = self.sbuf(ctx, "mod_tiles", [2 * 6 * KD, DEPTH, P])
            self.load("mod_c", [(CR[:, :, :], ins["c_columns"])] +
                      [(rows[:, layer, :], ins["b_ada"][layer:layer + 1, :].broadcast_to([2, NM]))
                       for layer in range(DEPTH)])
            sem = self.Sems(self, "mod_silu")
            cleared = sem("cleared")
            with nc.Block() as block:
                @block.vector
                def _(dve):
                    dve.memset(CP[:, :, :], 0.0).then_inc(cleared, 1)

                @block.scalar
                def _(act):
                    act.wait_ge(cleared, 1)
                    act.activation(CP[:, :, 0:2], CR[:, :, :], ACT.Silu)
            self.end(sem)
            self.split("mod_split", [(CP[:, :, :], CS[0][:, :, :], CS[1][:, :, :])])

            BLOCKS, UNIT, R, S = DEPTH * NM // BANK, KD * BANK // 2, 4, 4
            sem = self.Sems(self, "mod")
            raw_in = [sem(f"raw_in{u}") for u in range(R)]
            high, low, used, added = sem("high"), sem("low"), sem("used"), sem("added")
            WR = self.sbuf(ctx, "w_raw", [P, R, UNIT])
            WS = [self.sbuf(ctx, n, [P, S, UNIT], F32R) for n in ("w_high", "w_low")]
            rows_flat = rows[:, :, :].rearrange("v l n -> v (l n)")
            with nc.Block() as block:
                @block.sync
                def _(sp):
                    with sp.Fori(0, BLOCKS // 2) as i:
                        for u in range(R):
                            sp.wait_ge(low, i * R + u + 1)
                            sp.dma_start(WR[:, u, :], ins["w_ada"][bass.ds(i * 2 + u // 2, 1)].rearrange(
                                "e p n -> p (e n)")[:, u % 2 * UNIT:(u % 2 + 1) * UNIT]).then_inc(raw_in[u], 16)

                @block.scalar
                def _(act):
                    act.sem_inc(used, S)
                    with act.Fori(0, BLOCKS // 2) as i:
                        for u in range(R):
                            act.wait_ge(raw_in[u], i * 16 + 16)
                            act.wait_ge(used, i * R + u + 1)
                            act.copy(WS[0][:, u % S, :], WR[:, u, :]).then_inc(high, 1)

                @block.vector
                def _(dve):
                    dve.sem_inc(low, R)
                    dve.sem_inc(added, 2)

                    def add(i, b):
                        dve.wait_ge(used, i * R + (2 * b + 2 + S))
                        out = rows_flat[:, bass.ds(i * (2 * BANK) + b * BANK, BANK)]
                        dve.tensor_tensor(out, self.ps[0:2, b, :], out, ALU.add).then_inc(added, 1)

                    def body(i, first=False):
                        for u in range(R):
                            dve.wait_ge(high, i * R + u + 1)
                            dve.tensor_tensor(WS[1][:, u % S, :], WR[:, u, :], WS[0][:, u % S, :].bitcast(F32),
                                              ALU.subtract).then_inc(low, 1)
                            if u == 0 and not first:
                                add(i - 1, 1)
                            if u == 2:
                                add(i, 0)

                    body(0, first=True)
                    with dve.Fori(0, BLOCKS // 2 - 1) as i:
                        body(i + 1)
                    add(BLOCKS // 2 - 1, 1)

                @block.tensor
                def _(pe):
                    with pe.Fori(0, BLOCKS // 2) as i:
                        for u in range(R):
                            pe.wait_ge(low, i * R + (u + 1 + R))
                            if u % 2 == 0:
                                pe.wait_ge(added, i * 2 + (u // 2 + 1))
                            for k in range(KD // 2):
                                kk = u % 2 * (KD // 2) + k
                                for c, w in ((0, 0), (0, 1), (1, 0)):
                                    ins_ = pe.matmul(self.ps[:, u // 2, :], CS[c][:, kk, :],
                                                     WS[w][:, u % S, k * BANK:(k + 1) * BANK],
                                                     start=(kk == 0 and c + w == 0), stop=(kk == KD - 1 and c == 1))
                            ins_.then_inc(used, 1)
            self.end(sem)
            self.load("mod_out", [(self.mod[layer], rows[:, layer, :]) for layer in range(DEPTH)])
            self.load("mod_in", [(back[:, layer, :], self.mod[layer].rearrange("v (j p) -> (v j) p", p=P))
                                 for layer in range(DEPTH)])
            self.transpose("mod_T", [([back[:, layer, :]], self.MC[:, layer, :], None, None)
                                     for layer in range(DEPTH)])

    def modulated(self, name, layer, which, XT, tiles):
        nc, ins = self.nc, self.ins
        with ExitStack() as ctx:
            XN = self.sbuf(ctx, "xn", [P, tiles, DM])
            gain = self.sbuf(ctx, "gain", [P, KD])
            A = self.sbuf(ctx, "scale", [P, 2, KD])
            MC = self.MC[:, layer, :].rearrange("p (v j k) -> p v j k", v=2, j=6)
            self.norm(name + "_norm", [(self.H[:, t, :] if t < NT else self.C[:, t - NT, :], XN[:, t, :], None, None)
                                       for t in range(tiles)], "rms", RMS_EPS,
                      [(gain[:, :], ins[("norm_mix_g", "norm_ffn_g")[which]][layer])])
            sem = self.Sems(self, name + "_scale")
            step = sem("step")
            with nc.Block() as block:
                @block.vector
                def _(dve):
                    order = Order(dve, step)
                    for v in range(2):
                        order.done(dve.scalar_tensor_tensor(out=A[:, v, :], in0=MC[:, v, 3 * which + 1, :], scalar=1.0,
                                                            in1=gain[:, :], op0=ALU.add, op1=ALU.mult))
            self.end(sem)
            self.transpose_rows(name + "_T", XN, NT, XT, A[:, 0, :], MC[:, 0, 3 * which, :])
            if tiles > NT:
                self.transpose_rows(name + "_Tc", XN[:, NT:, :], NTC, XT, A[:, 1, :], MC[:, 1, 3 * which, :], at=T)

    def token_rows_of(self, t):
        return self.H[:, t, :] if t < NT else self.C[:, t - NT, :]

    def gates(self, ctx, name, layer, part, vectors):
        G = self.sbuf(ctx, "gates", [P, vectors, DM])
        self.load(name, [(G[:, v, :], self.mod[layer][v:v + 1, part * DM:(part + 1) * DM].broadcast_to([P, DM]))
                         for v in range(vectors)])
        return G

    def mixer_layer(self, layer):
        nc, ins = self.nc, self.ins
        last = layer == DEPTH - 1
        upd = NT if last else NTT
        with ExitStack() as outer:
            MX = self.sbuf(outer, "mixT", [P, KD, T + TC])
            UG = self.sbuf(outer, "u_gla", [P, NTT, 2 * QK + GV + 2 * GLA_LR])
            UR = self.sbuf(outer, "u_r", [P, upd, GV])
            LR = self.sbuf(outer, "lowrankT", [GLA_LR + 1, 2, T + TC])
            with ExitStack() as ctx:
                UV = self.sbuf(ctx, "u_nav", [P, NTT, NA_H * DH])
                SC = self.sbuf(ctx, "scT", [P, 6, upd * P])
                NQ = self.sbuf(ctx, "naqT", [P, 3, upd * P])
                NK = self.sbuf(ctx, "nakT", [P, 3, T + TC])
                with ExitStack() as c2:
                    self.modulated(f"x{layer}", layer, 0, MX, NTT)
                with ExitStack() as c2:
                    sem = self.Sems(self, f"ones{layer}")
                    set_ = sem("set")
                    with nc.Block() as block:
                        @block.gpsimd
                        def _(pool):
                            pool.memset(LR[:, :, :], 1.0).then_inc(set_, 1)
                            pool.wait_ge(set_, 1)
                    self.end(sem)
                    blocks = [self.rows_block(ins[w][layer], n, tiles, lambda t, o=out: o[:, t, :],
                                              lambda t: ("copy", None))
                              for w, n, out, tiles in (("w_qk", 2 * QK, UG[:, :, 0:2 * QK], NTT),
                                                       ("w_v_lr", GV + 2 * GLA_LR, UG[:, :, 2 * QK:], NTT),
                                                       ("w_r", GV, UR, upd), ("w_nav", NA_H * DH, UV, NTT))]
                    dests = [(SC[:, j, :], not last, None) for j in range(6)] + \
                            [(NQ[:, j, :], not last, DH ** -0.5) for j in range(3)] + \
                            [(NK[:, j, :], True, None) for j in range(3)]
                    for c in range(3):
                        blocks.append((ins["w_cols"][layer, c], BANK, True, [
                            ((j * P, (j + 1) * P), (x, y), dests[4 * c + j][0][:, x:y], ("copy", dests[4 * c + j][2]))
                            for j in range(4)
                            for x, y in ((0, T), (T, T + TC))[:2 if dests[4 * c + j][1] else 1]]))
                    self.stream(f"u{layer}", MX[:, :, :], KD, blocks)
                    self.transpose(f"lrT{layer}", [
                        ([UG[:, t, 2 * QK + GV + d * GLA_LR:2 * QK + GV + (d + 1) * GLA_LR] for t in range(a, b)],
                         LR[0:GLA_LR, d, a * P:b * P], None, None)
                        for d in range(2) for a, b in ((0, NT), (NT, NTT))])
                self.short_convolution(layer, SC, MX, upd)
                with ExitStack() as c2:
                    NO = self.sbuf(c2, "na_rows", [P, upd, NA_H * DH])
                    self.neighbourhood(layer, NQ, NK, UV, NO, last)
                    groups = []
                    for k in range(3):
                        for a in range(0, upd, 4):
                            b = min(a + 4, upd)
                            groups.append(([NO[:, t, k * P:(k + 1) * P] for t in range(a, b)],
                                           MX[:, 5 + k, a * P:b * P], None, None))
                    self.transpose(f"naT{layer}", groups)
            self.gated_linear(layer, UG, UR, LR, MX, upd)
            with ExitStack() as ctx:
                G = self.gates(ctx, f"g1_{layer}", layer, 2, 1 if last else 2)
                self.stream(f"wout{layer}", MX[:, :, 0:upd * P], KD, [
                    self.rows_block(ins["w_out"][layer, c], BANK, upd,
                                    lambda t, c=c: self.token_rows_of(t)[:, c * BANK:(c + 1) * BANK],
                                    lambda t, c=c: ("gated", G[:, t // NT, c * BANK:(c + 1) * BANK]))
                    for c in range(2)])

    def short_convolution(self, layer, SC, MX, upd):
        nc = self.nc
        with ExitStack() as ctx:
            sem = self.Sems(self, f"sc{layer}")
            step = sem("step")
            w_in = sem("w_in")
            W = self.sbuf(ctx, "sc_w", [P, 2, 4])
            segs = [(0, T), (T, upd * P)][:1 if upd == NT else 2]
            with nc.Block() as block:
                @block.sync
                def _(sp):
                    sp.dma_start(W[:, :, :], self.ins["sc_conv"][layer]).then_inc(w_in, 16)

                @block.vector
                def _(dve):
                    order = Order(dve, step)
                    dve.wait_ge(w_in, 16)
                    for j in range(2):
                        x, o = SC[:, 4 + j, :], MX[:, 3 + j, 0:upd * P]
                        order.done(dve.tensor_tensor(x, x, SC[:, 2 + j, :], ALU.mult))
                        order.done(dve.tensor_scalar(o, x, W[:, j, 1:2], W[:, j, 3:4], ALU.mult, ALU.add))
                        for a, b in segs:
                            order.done(dve.scalar_tensor_tensor(out=o[:, a + 1:b], in0=x[:, a:b - 1], scalar=W[:, j, 0:1],
                                                                in1=o[:, a + 1:b], op0=ALU.mult, op1=ALU.add))
                            order.done(dve.scalar_tensor_tensor(out=o[:, a:b - 1], in0=x[:, a + 1:b], scalar=W[:, j, 2:3],
                                                                in1=o[:, a:b - 1], op0=ALU.mult, op1=ALU.add))
                        order.done(dve.tensor_tensor(o, o, SC[:, j, :], ALU.mult))
            self.end(sem)

    def neighbourhood(self, layer, NQ, NK, UV, NO, last):
        nc, ins = self.nc, self.ins
        ROWS, COLS, NJ = 2 * 8 - 1, 2 * GRID_W - 1, 14
        with ExitStack() as ctx:
            RB = self.sbuf(ctx, "rel_bias", [P, NA_H, NJ, GRID_W])
            src = ins["rpb_padded"]
            pairs = []
            for r in range(2):
                for h in range(NA_H):
                    off = src[layer, h].offset + (1 - r) * COLS
                    pairs.append((RB[r * GRID_W:(r + 1) * GRID_W, h],
                                  bass.AP(src.tensor, off, [[1, GRID_W], [COLS, NJ], [1, GRID_W]])))
            self.load(f"rb{layer}", pairs)
            sem = self.Sems(self, f"rbm{layer}")
            step = sem("step")
            with nc.Block() as block:
                @block.vector
                def _(dve):
                    order = Order(dve, step)
                    v = RB[:, :, :, :].rearrange("p h j c -> p (h j) c")
                    order.done(dve.tensor_tensor(v, v, self.const("columns")[:, ::-1].unsqueeze(1).broadcast_to(
                        [P, NA_H * NJ, GRID_W]), ALU.add))
            self.end(sem)
            units = []
            for t in range(NT):
                for h in range(NA_H):
                    r = (h % 2) * DH
                    j = 6 - 2 * t
                    units.append((NQ[r:r + DH, h // 2, t * P:(t + 1) * P],
                                  [NK[r:r + DH, h // 2, 0:T], NK[r:r + DH, h // 2, T:T + TC]],
                                  [RB[:, h, j:j + 8, ::-1], TC], None,
                                  [UV[:, c, h * DH:(h + 1) * DH] for c in range(NTT)],
                                  NO[:, t, h * DH:(h + 1) * DH]))
            if not last:
                for t in range(NT, NTT):
                    for h in range(NA_H):
                        r = (h % 2) * DH
                        units.append((NQ[r:r + DH, h // 2, t * P:(t + 1) * P], [NK[r:r + DH, h // 2, T:T + TC]],
                                      [TC], None, [UV[:, c, h * DH:(h + 1) * DH] for c in range(NT, NTT)],
                                      NO[:, t, h * DH:(h + 1) * DH]))
            self.attention(f"na{layer}", units, DH)

    def gated_linear(self, layer, UG, UR, LR, MX, upd):
        nc, ins = self.nc, self.ins
        NC8 = P // CHUNK
        SL = NCH + 1
        NL = T // CHUNK
        def slot(d, c):
            lat = c < NL
            if d == 0:
                return NCH - NL + c if lat else c - NL
            return NCH - 1 - c if lat else NCH - 1 - c
        with ExitStack() as outer:
            ON = self.sbuf(outer, "gla_rows", [P, upd, GV])
            with ExitStack() as ctx:
                KE = self.sbuf(ctx, "k_end", [P, NTT, 2, QK])
                QD = self.sbuf(ctx, "q_dec", [P, NTT, 2, QK])
                KI = self.sbuf(ctx, "k_inv", [P, NTT, 2, QK])
                DEC = self.sbuf(ctx, "decay", [HG * GLA_DK, 2, 2, SL])
                with ExitStack() as c2:
                    G = self.sbuf(c2, "log_gate", [P, NTT, 2 * QK])
                    with ExitStack() as c3:
                        ring = self.sbuf(c3, "ring", [P, 1, 2 * QK])
                        self.project(f"z{layer}", ring, [(ins["gla_wg2"][layer], [
                            (G[:, t, d * QK:(d + 1) * QK],
                             [(LR[:, d, t * P:(t + 1) * P], ring[0:GLA_LR + 1, 0, d * QK:(d + 1) * QK])],
                             ("copy", None)) for t in range(NTT) for d in range(2)])])
                    nh, half = 2 * GLA_H, GLA_DK // 2
                    cos = self.const("rope_g_cos").rearrange("p (t d) -> p t d", t=NT)
                    sin = self.const("rope_g_sin").rearrange("p (t d) -> p t d", t=NT)
                    with ExitStack() as c3:
                        tm = self.sbuf(c3, "rope_tmp", [P, 3, nh, half])
                        jobs = []
                        for t in range(NT):
                            x = UG[:, t, 0:2 * QK].rearrange("p (h d two) -> p h d two", h=nh, two=2)
                            bc = lambda a: a[:, t, :].unsqueeze(1).broadcast_to([P, nh, half])
                            jobs.append((x[:, :, :, 0], x[:, :, :, 1], bc(cos), bc(sin), tm[:, 0], tm[:, 1], tm[:, 2]))
                        self.rope_halves(f"rope_g{layer}", jobs)
                    self.decays(layer, UG, G, QD, KI, KE, DEC, slot, SL)
                for grp in range(2):
                    self.gla_group(layer, grp, UG, QD, KI, KE, DEC, ON, upd, slot, SL)
            self.gla_output(layer, ON, UR, upd)
            groups = []
            for k in range(3):
                for a in range(0, upd, 4):
                    b = min(a + 4, upd)
                    groups.append(([ON[:, t, k * P:(k + 1) * P] for t in range(a, b)],
                                   MX[:, k, a * P:b * P], None, None))
            self.transpose(f"glaT{layer}", groups)

    def decays(self, layer, UG, G, QD, KI, KE, DEC, slot, SL):
        nc = self.nc
        NC8 = P // CHUNK
        with ExitStack() as ctx:
            sem = self.Sems(self, f"dec{layer}")
            (abs_done, ln_done, g_done, sums, exps, multiplied, dec_sums, dec_out, zeroed, vstep, astep) = (sem(n) for n in (
                "abs", "ln", "gates", "sums", "exps", "multiplied", "dec_sums", "dec_out", "zeroed", "vstep", "astep"))
            A = self.sbuf(ctx, "abs", [P, NTT, 2 * QK])
            E = self.sbuf(ctx, "exps", [P, 2, 3, 2 * QK])
            DP = self.ps[0:HG * GLA_DK, 4, 0:4 * NCH].rearrange("p (d g c) -> p d g c", d=2, g=2)
            BP = lambda t: self.ps[:, 2 * (t % 2), 0:2 * QK]
            EP = lambda t: self.ps[:, 2 * (t % 2) + 1, 0:2 * QK]
            with nc.Block() as block:
                @block.vector
                def _(dve):
                    order = Order(dve, vstep)
                    dve.memset(DEC[:, :, :, :], 0.0).then_inc(zeroed, 1)
                    g_flat, a_flat = (x[:, :, :].rearrange("p t n -> p (t n)") for x in (G, A))
                    dve.scalar_tensor_tensor(out=a_flat, in0=g_flat, scalar=-1.0, in1=g_flat,
                                             op0=ALU.mult, op1=ALU.max).then_inc(abs_done, 1)
                    dve.wait_ge(ln_done, 1)
                    dve.scalar_tensor_tensor(out=g_flat, in0=g_flat, scalar=0.0, in1=a_flat,
                                             op0=ALU.min, op1=ALU.subtract).then_inc(g_done, 1)
                    for t in range(NTT):
                        dve.wait_ge(exps, t + 1)
                        b = t % 2
                        for d in range(2):
                            c = slice(d * QK, (d + 1) * QK)
                            order.done(dve.scalar_tensor_tensor(out=QD[:, t, d, :], in0=E[:, b, 0, c],
                                       scalar=GLA_DK ** -0.5, in1=UG[:, t, 0:QK], op0=ALU.mult, op1=ALU.mult))
                            order.done(dve.tensor_tensor(KI[:, t, d, :], E[:, b, 1, c], UG[:, t, QK:2 * QK], ALU.mult))
                            ins_ = dve.tensor_tensor(KE[:, t, d, :], E[:, b, 2, c], UG[:, t, QK:2 * QK], ALU.mult)
                            if d == 0:
                                order.done(ins_)
                            else:
                                ins_.then_inc(multiplied, 1)
                    dve.wait_ge(multiplied, NTT)

                @block.scalar
                def _(act):
                    act.wait_ge(abs_done, 1)
                    act.activation(A[:, :, :], A[:, :, :], ACT.Exp, scale=-1.0).then_inc(astep, 1)
                    act.wait_ge(astep, 1)
                    act.activation(A[:, :, :], A[:, :, :], ACT.Ln, bias=1.0).then_inc(ln_done, 1)
                    for t in range(NTT):
                        act.wait_ge(sums, t + 1)
                        if t >= 2:
                            act.wait_ge(multiplied, t - 1)
                        b = t % 2
                        act.activation(E[:, b, 0, :], BP(t), ACT.Exp).then_inc(astep, 1)
                        act.activation(E[:, b, 1, :], BP(t), ACT.Exp, scale=-1.0).then_inc(astep, 1)
                        act.wait_ge(astep, 3 + 2 * t)
                        act.activation(E[:, b, 2, :], EP(t), ACT.Exp).then_inc(exps, 1)
                    act.wait_ge(dec_sums, 1)
                    act.wait_ge(zeroed, 1)
                    for d in range(2):
                        for g in range(2):
                            for lat in range(2):
                                c0, n = (0, T // CHUNK) if lat else (T // CHUNK, TC // CHUNK)
                                s0 = slot(d, c0) + 1
                                dst = DEC[:, d, g, s0:s0 + n] if d == 0 else DEC[:, d, g, s0 - n + 1:s0 + 1][:, ::-1]
                                act.activation(dst, DP[:, d, g, c0:c0 + n], ACT.Exp).then_inc(dec_out, 1)
                    act.wait_ge(dec_out, 8)

                @block.tensor
                def _(pe):
                    pe.wait_ge(g_done, 1)
                    for t in range(NTT):
                        if t >= 2:
                            pe.wait_ge(exps, t - 1)
                        for n, (name, d) in enumerate((("sum_upto", 0), ("sum_from", 1),
                                                       ("sum_after", 0), ("sum_before", 1))):
                            out = (BP(t), EP(t))[n // 2][:, d * QK:(d + 1) * QK]
                            ins_ = pe.matmul(out, self.const(name), G[:, t, d * QK:(d + 1) * QK], start=True, stop=True)
                        ins_.then_inc(sums, 1)
                    for d in range(2):
                        for g in range(2):
                            a = d * QK + g * HG * GLA_DK
                            for t in range(NTT):
                                ins_ = pe.matmul(DP[:, d, g, t * NC8:(t + 1) * NC8], G[:, t, a:a + HG * GLA_DK],
                                                 self.const("chunk_tau"), start=True, stop=True)
                    ins_.then_inc(dec_sums, 1)
            self.end(sem)

    def gla_group(self, layer, grp, UG, QD, KI, KE, DEC, ON, upd, slot, SL):
        nc = self.nc
        NC8, W3 = P // CHUNK, HG * GLA_DK
        cols = slice(grp * W3, (grp + 1) * W3)
        name = f"gla{layer}{grp}"
        V = lambda t, hh: UG[:, t, 2 * QK + (grp * HG + hh) * GLA_DV:2 * QK + (grp * HG + hh + 1) * GLA_DV]
        with ExitStack() as ctx:
            QT = self.sbuf(ctx, "q_decT", [W3, 2, upd * P])
            KT = self.sbuf(ctx, "k_invT", [W3, 2, upd * P])
            QB = self.sbuf(ctx, "q_blocks", [W3, 2, upd * NC8, HG, CHUNK])
            ST = self.sbuf(ctx, "states", [W3, 2, GLA_DV, SL])
            DX = self.sbuf(ctx, "decay_wide", [W3, GLA_DV, SL])
            OT = DX[0:GLA_DV, :, :].rearrange("p v s -> p (v s)")[:, 0:HG * upd * P].rearrange(
                "p (h n) -> p h n", h=HG)
            groups = []
            for d in range(2):
                for src, dst in ((QD, QT), (KI, KT)):
                    for a in range(0, upd, 4):
                        b = min(a + 4, upd)
                        groups.append(([src[:, t, d, cols] for t in range(a, b)], dst[:, d, a * P:b * P], None, None))
            self.transpose(name + "T", groups)

            sem = self.Sems(self, name)
            expanded = [sem("expanded_by_pool"), sem("expanded_by_dve")]
            (updates, up_out_v, up_out_a, cleared, zeroed, blocked, dec_done, scanned, scored, masked, mixed, out_done) = (
                sem(n) for n in ("updates", "up_out_v", "up_out_a", "cleared", "zeroed", "blocked", "dec_done",
                                 "scanned", "scored", "masked", "mixed", "out_done"))
            with ExitStack() as c2:
                VX = self.sbuf(c2, "v_chunks", [P, 2, NC8, GLA_DV])
                AT = self.sbuf(c2, "scoresT", [P, 2, HG, 2, P])
                UB = lambda t, d: self.ps[0:W3, 2 * (t % 2) + d, :]
                masks = self.consts[:, self.const_at["upto"][0]:self.const_at["upto"][0] + 2 * P].rearrange(
                    "p (d n) -> p d n", d=2)
                SB = lambda hh: self.ps[:, hh, 0:2 * P]
                OB = lambda t: self.ps[0:GLA_DV, 6 + t % 2, 0:HG * P].rearrange("p (h n) -> p h n", h=HG)

                def expand(eng, n):
                    if n >= 2:
                        eng.wait_ge(updates, n - 1)
                    eng.tensor_tensor(VX[:, n % 2], V(n // HG, n % HG).unsqueeze(1).broadcast_to([P, NC8, GLA_DV]),
                                      self.const("chunk").unsqueeze(2).broadcast_to([P, NC8, GLA_DV]),
                                      ALU.mult).then_inc(expanded[n % 2], 1)

                with nc.Block() as block:
                    @block.gpsimd
                    def _(pool):
                        for n in range(0, NTT * HG, 2):
                            expand(pool, n)
                        pool.memset(QB[:, :, :, :, :], 0.0).then_inc(cleared, 1)
                        pool.wait_ge(cleared, 1)
                        for d in range(2):
                            for hh in range(HG):
                                r = slice(hh * GLA_DK, (hh + 1) * GLA_DK)
                                pool.tensor_copy(QB[r, d, :, hh, :], QT[r, d, :].rearrange(
                                    "p (c n) -> p c n", n=CHUNK)).then_inc(blocked, 1)

                    @block.tensor
                    def _(pe):
                        for t in range(NTT):
                            if t >= 2:
                                pe.wait_ge(up_out_v, t - 1)
                                pe.wait_ge(up_out_a, t - 1)
                            for hh in range(HG):
                                n = t * HG + hh
                                pe.wait_ge(expanded[n % 2], n // 2 + 1)
                                for d in range(2):
                                    h = grp * HG + hh
                                    ins_ = pe.matmul(UB(t, d)[hh * GLA_DK:(hh + 1) * GLA_DK, :],
                                                     KE[:, t, d, h * GLA_DK:(h + 1) * GLA_DK],
                                                     VX[:, n % 2].rearrange("p c v -> p (c v)"), start=True, stop=True)
                                ins_.then_inc(updates, 1)

                        def scores(t):
                            if t == 0:
                                pe.wait_ge(up_out_v, NTT)
                                pe.wait_ge(up_out_a, NTT)
                            else:
                                pe.wait_ge(masked, HG * t)
                            for hh in range(HG):
                                r = slice(hh * GLA_DK, (hh + 1) * GLA_DK)
                                for d in range(2):
                                    ins_ = pe.matmul(SB(hh)[:, d * P:(d + 1) * P], KT[r, d, t * P:(t + 1) * P],
                                                     QT[r, d, t * P:(t + 1) * P], start=True, stop=True)
                                ins_.then_inc(scored, 1)

                        def mix(t):
                            pe.wait_ge(masked, HG * (t + 1))
                            if t >= 2:
                                pe.wait_ge(out_done, t - 1)
                            for hh in range(HG):
                                for d in range(2):
                                    pe.matmul(OB(t)[:, hh, :], V(t, hh), AT[:, t % 2, hh, d, :],
                                              start=(hh == 0 and d == 0), stop=False, skip_group_check=True)
                            if t == 0:
                                pe.wait_ge(scanned, 2)
                                pe.wait_ge(blocked, 2 * HG)
                            for d in range(2):
                                for c in range(NC8):
                                    ch = t * NC8 + c
                                    ins_ = pe.matmul(OB(t)[:, :, c * CHUNK:(c + 1) * CHUNK],
                                                     ST[:, d, :, slot(d, ch)], QB[:, d, ch],
                                                     start=False, stop=(d == 1 and c == NC8 - 1), skip_group_check=True)
                            ins_.then_inc(mixed, 1)

                        scores(0)
                        for t in range(upd):
                            if t + 1 < upd:
                                scores(t + 1)
                            mix(t)

                    @block.vector
                    def _(dve):
                        def place_updates(eng, t, d):
                            s0 = slot(d, t * NC8) + 1
                            dst = ST[:, d, :, s0:s0 + NC8] if d == 0 else ST[:, d, :, s0 - NC8 + 1:s0 + 1][:, :, ::-1]
                            return eng(dst, UB(t, d).rearrange("p (c v) -> p v c", v=GLA_DV))

                        dve.memset(ST[:, :, :, 0:1], 0.0).then_inc(zeroed, 1)
                        for t in range(NTT + 1):
                            for n in range(t * HG, min(t + 1, NTT) * HG):
                                if n % 2:
                                    expand(dve, n)
                            if t:
                                dve.wait_ge(updates, HG * t)
                                place_updates(dve.tensor_copy, t - 1, 0).then_inc(up_out_v, 1)
                        for d in range(2):
                            if d == 1:
                                dve.wait_ge(scanned, 1)
                            dve.tensor_copy(DX[:, :, :], DEC[:, d, grp, :].unsqueeze(1).broadcast_to(
                                [W3, GLA_DV, SL])).then_inc(dec_done, 1)
                            dve.wait_ge(dec_done, d + 1)
                            dve.wait_ge(zeroed, 1)
                            dve.wait_ge(up_out_v, NTT)
                            dve.wait_ge(up_out_a, NTT)
                            flat = ST[:, d, :, :].rearrange("p v s -> p (v s)")
                            dve.tensor_tensor_scan(flat, DX[:, :, :].rearrange("p v s -> p (v s)"), flat, 0.0,
                                                   ALU.mult, ALU.add).then_inc(scanned, 1)
                        for t in range(upd):
                            for hh in range(HG):
                                dve.wait_ge(scored, HG * t + hh + 1)
                                if t >= 2:
                                    dve.wait_ge(mixed, t - 1)
                                dve.tensor_tensor(AT[:, t % 2, hh], SB(hh).rearrange("p (d n) -> p d n", d=2), masks,
                                                  ALU.mult).then_inc(masked, 1)

                    @block.scalar
                    def _(act):
                        for t in range(NTT):
                            act.wait_ge(updates, HG * (t + 1))
                            s0 = slot(1, t * NC8) + 1
                            act.copy(ST[:, 1, :, s0 - NC8 + 1:s0 + 1][:, :, ::-1],
                                     UB(t, 1).rearrange("p (c v) -> p v c", v=GLA_DV)).then_inc(up_out_a, 1)
                        for t in range(upd):
                            act.wait_ge(mixed, t + 1)
                            act.copy(OT[:, :, t * P:(t + 1) * P], OB(t)).then_inc(out_done, 1)
                self.end(sem)
            W = HG * GLA_DV
            self.transpose(name + "oT", [([OT[:, hh, t * P:(t + 1) * P] for hh in range(HG)],
                                          ON[:, t, grp * W:(grp + 1) * W], None, None) for t in range(upd)])

    def gla_output(self, layer, ON, UR, upd):
        nc = self.nc
        with ExitStack() as ctx:
            sem = self.Sems(self, f"go{layer}")
            gain_in, squared, rooted, gated, step = (sem(n) for n in ("gain_in", "squared", "rooted", "gated", "step"))
            gain = self.sbuf(ctx, "gain", [P, GLA_DV])
            sq = self.sbuf(ctx, "squares", [P, upd, GV])
            ms = self.sbuf(ctx, "ms", [P, 3, upd * GLA_H])
            eps_t = self.sbuf(ctx, "eps", [P, 1])
            n = upd * GLA_H
            heads = lambda a: a[:, :, :].rearrange("p t (h v) -> p (t h) v", v=GLA_DV)
            with nc.Block() as block:
                @block.sync
                def _(sp):
                    sp.dma_start(gain[:, :], self.ins["gla_norm_g"][layer:layer + 1, :].broadcast_to(
                        [P, GLA_DV])).then_inc(gain_in, 16)

                @block.vector
                def _(dve):
                    order = Order(dve, step)
                    order.done(dve.memset(eps_t[:, :], RMS_EPS))
                    order.done(dve.tensor_tensor(sq[:, :, :], ON[:, :, :], ON[:, :, :], ALU.mult))
                    dve.tensor_reduce(ms[:, 0, :], heads(sq), AX_X, ALU.add).then_inc(squared, 1)
                    dve.wait_ge(rooted, 1)
                    order.done(dve.reciprocal(ms[:, 2, :], ms[:, 1, :]))
                    order.done(dve.tensor_tensor(heads(ON), heads(ON), ms[:, 2, :].unsqueeze(2).broadcast_to(
                        [P, n, GLA_DV]), ALU.mult))
                    dve.wait_ge(gain_in, 16)
                    order.done(dve.tensor_tensor(heads(ON), heads(ON), gain[:, :].unsqueeze(1).broadcast_to(
                        [P, n, GLA_DV]), ALU.mult))
                    dve.wait_ge(gated, 1)
                    order.done(dve.tensor_tensor(ON[:, :, :], ON[:, :, :], UR[:, 0:upd, :], ALU.mult))

                @block.scalar
                def _(act):
                    act.activation(UR[:, 0:upd, :], UR[:, 0:upd, :], ACT.Silu).then_inc(gated, 1)
                    act.wait_ge(squared, 1)
                    act.wait_ge(step, 1)
                    act.activation(ms[:, 1, :], ms[:, 0, :], ACT.Sqrt, scale=1.0 / GLA_DV,
                                   bias=eps_t[:, :]).then_inc(rooted, 1)
            self.end(sem)

    def ffn_layer(self, layer):
        nc, ins = self.nc, self.ins
        last = layer == DEPTH - 1
        tiles = NT if last else NTT
        ntok = tiles * P
        segs = [(0, T), (T, ntok)][:1 if last else 2]
        with ExitStack() as ctx:
            AT = self.sbuf(ctx, "hiddenT", [P, NF, ntok])
            with ExitStack() as c2:
                XS = [self.sbuf(c2, n, [P, KD, ntok], F32R) for n in ("x_high", "x_low")]
                with ExitStack() as c3:
                    XT = self.sbuf(c3, "xT", [P, KD, ntok])
                    self.modulated(f"f{layer}", layer, 1, XT, tiles)
                    self.split(f"f{layer}_split", [(XT[:, k, :], XS[0][:, k, :], XS[1][:, k, :])
                                                   for k in range(KD)])
                self.ffn_up(layer, XS, AT, ntok, segs)
            with ExitStack() as c2:
                G = self.gates(c2, f"g2_{layer}", layer, 5, 1 if last else 2)
                self.stream(f"down{layer}", AT[:, :, :], NF, [
                    self.rows_block(ins["ffn_w_down"][layer, c], BANK, tiles,
                                    lambda t, c=c: self.token_rows_of(t)[:, c * BANK:(c + 1) * BANK],
                                    lambda t, c=c: ("gated", G[:, t // NT, c * BANK:(c + 1) * BANK]))
                    for c in range(2)])

    def ffn_up(self, layer, XS, AT, ntok, segs):
        nc, ins = self.nc, self.ins
        UNIT = KD * 2 * P
        with ExitStack() as ctx:
            sem = self.Sems(self, f"up{layer}")
            raw_in, taps_in = sem("raw_in"), sem("taps_in")
            high, low, multiplied = sem("high"), sem("low"), sem("multiplied")
            centred, convolved, gated, left, step = (sem(n) for n in ("centred", "convolved", "gated", "left", "step"))
            W = self.sbuf(ctx, "w_raw", [P, UNIT])
            WS = [self.sbuf(ctx, n, [P, 2, UNIT], F32R) for n in ("w_high", "w_low")]
            CV = self.sbuf(ctx, "taps", [P, NF, 2, 4])
            cv = CV[:, :, :, :].rearrange("p f a w -> p (f a w)")
            Z = self.sbuf(ctx, "convolved", [P, 2, ntok])
            GA = self.sbuf(ctx, "silu", [P, ntok])
            U = lambda b, ab: self.ps[:, 4 * b + 2 * ab:4 * b + 2 * ab + 2, :].rearrange("p b n -> p (b n)")

            def tiles(eng, tile):
                with eng.Fori(0, NF // 2 - 1) as i:
                    for b in range(2):
                        tile(i * 2 + b, b)
                for b in range(2):
                    tile(NF - 2 + b, b)

            with nc.Block() as block:
                @block.sync
                def _(sp):
                    sp.dma_start(CV[:, :, :, :], ins["ffn_conv"][layer]).then_inc(taps_in, 16)

                    def tile(f, b):
                        sp.wait_ge(low, f + 1)
                        sp.dma_start(W[:, :], ins["ffn_w_up"][bass.ds(f + layer * NF, 1)].rearrange(
                            "e p n -> p (e n)")).then_inc(raw_in, 16)
                    tiles(sp, tile)

                @block.tensor
                def _(pe):
                    pe.sem_inc(multiplied, 2)

                    def tile(f, b):
                        pe.wait_ge(low, f + 2)
                        pe.wait_ge(convolved, f + 1)
                        for ab in range(2):
                            for k in range(KD):
                                for first, second in ((0, 0), (0, 1), (1, 0)):
                                    for x, y in segs:
                                        at = (2 * k + ab) * P
                                        ins_ = pe.matmul(U(b, ab)[:, x:y], WS[first][:, b, at:at + P],
                                                         XS[second][:, k, x:y],
                                                         start=(k == 0 and first + second == 0),
                                                         stop=(k == KD - 1 and first == 1))
                        ins_.then_inc(multiplied, 1)
                    tiles(pe, tile)

                @block.scalar
                def _(act):
                    act.wait_ge(taps_in, 16)

                    def raise_(f, b):
                        act.wait_ge(raw_in, f * 16 + 16)
                        act.wait_ge(multiplied, f + 1)
                        act.copy(WS[0][:, b, :], W[:, :]).then_inc(high, 1)

                    raise_(0, 0)
                    act.sem_inc(gated, 1)

                    def tile(f, b):
                        if not (isinstance(f, int) and f == NF - 1):
                            raise_(f + 1, 1 - b)
                        act.wait_ge(multiplied, f + 3)
                        act.wait_ge(left, f + 1)
                        for ab in range(2):
                            act.activation(Z[:, ab, :], U(b, ab)[:, 0:ntok], ACT.Identity,
                                           bias=cv[:, bass.ds(f * 8 + (4 * ab + 3), 1)],
                                           scale=cv[:, bass.ds(f * 8 + (4 * ab + 1), 1)]).then_inc(centred, 1)
                        act.wait_ge(convolved, f + 3)
                        act.activation(GA[:, :], Z[:, 0, :], ACT.Silu).then_inc(gated, 1)
                    tiles(act, tile)

                @block.vector
                def _(dve):
                    dve.sem_inc(low, 1)
                    dve.sem_inc(convolved, 2)
                    dve.sem_inc(left, 1)

                    def lower(f, b):
                        dve.wait_ge(high, f + 1)
                        dve.tensor_tensor(WS[1][:, b, :], W[:, :], WS[0][:, b, :].bitcast(F32),
                                          ALU.subtract).then_inc(low, 1)

                    lower(0, 0)

                    def tile(f, b):
                        if not (isinstance(f, int) and f == NF - 1):
                            lower(f + 1, 1 - b)
                        for ab in range(2):
                            dve.wait_ge(centred, f * 2 + (ab + 1))
                            z, u = Z[:, ab, :], U(b, ab)
                            for x, y in segs:
                                dve.scalar_tensor_tensor(out=z[:, x + 1:y], in0=u[:, x:y - 1],
                                                         scalar=cv[:, bass.ds(f * 8 + 4 * ab, 1)],
                                                         in1=z[:, x + 1:y], op0=ALU.mult,
                                                         op1=ALU.add).then_inc(step, 1)
                            dve.wait_ge(step, (f * 2 + (ab + 1)) * len(segs))
                            for x, y in segs:
                                ins_ = dve.scalar_tensor_tensor(out=z[:, x:y - 1], in0=u[:, x + 1:y],
                                                                scalar=cv[:, bass.ds(f * 8 + (4 * ab + 2), 1)],
                                                                in1=z[:, x:y - 1], op0=ALU.mult, op1=ALU.add)
                        ins_.then_inc(convolved, 1)
                        dve.wait_ge(gated, f + 2)
                        dve.wait_ge(convolved, f + 3)
                        dve.tensor_tensor(AT[:, bass.ds(f, 1), :].rearrange("p e n -> p (e n)"), GA[:, :],
                                          Z[:, 1, :], ALU.mult).then_inc(left, 1)
                    tiles(dve, tile)
            self.end(sem)

    def finish(self):
        with ExitStack() as ctx:
            g = self.sbuf(ctx, "gain", [P, DM])
            self.norm("final", [(self.H[:, t, :], self.H[:, t, :], g[:, :], None) for t in range(NT)], "rms", RMS_EPS,
                      [(g[:, :], self.ins["final_norm_g"].broadcast_to([P, DM]))])
            self.load("store", [(self.out[t * P:(t + 1) * P, :], self.H[:, t, :]) for t in range(NT)])


    def build(self):
        nc = self.nc
        with ExitStack() as ctx:
            self.ps = ctx.enter_context(nc.psum_tensor("banks", [P, 8, BANK], F32))
            self.const_at, table = constant_columns()
            self.consts = ctx.enter_context(nc.sbuf_tensor("consts", [P, table.shape[1]], F32))
            self.H = ctx.enter_context(nc.sbuf_tensor("H", [P, NT, DM], F32))
            self.C = C = ctx.enter_context(nc.sbuf_tensor("C", [P, NTC, DM], F32))
            self.sinks = ctx.enter_context(nc.sbuf_tensor("sinks", [P, A_HEADS], F32))
            self.load("start", [(self.consts[:, :], self.ins["consts"]),
                                (self.H[:, :, :], self.ins["x"].rearrange("(t p) d -> p t d", p=P)),
                                (C[:, :, :], self.ins["ctx"].rearrange("(t p) d -> p t d", p=P)),
                                (self.sinks[:, :], self.ins["a_sinks"].broadcast_to([P, A_HEADS]))])
            self.rows = nc.dram_tensor("token_rows", (T, DM), F32).ap()
            self.table = [nc.dram_tensor(f"slot_table{i}", (EXPERTS * T, 1), I32).ap() for i in range(DEPTH)]
            self.Y = [nc.dram_tensor(f"expert_rows{i}", (2 * T, DM), F32).ap() for i in range(DEPTH)]
            self.mod = [nc.dram_tensor(f"mod_rows{i}", (2, 6 * DM), F32).ap() for i in range(DEPTH)]
            self.MC = ctx.enter_context(nc.sbuf_tensor("MC", [P, DEPTH, 2 * 6 * KD], F32))
            self.window_layer()
            self.moe_layer(0)
            self.latent_layer()
            self.moe_layer(1)
            self.second_block()
            self.finish()

    def second_block(self):
        self.modulation()
        for layer in range(DEPTH):
            self.mixer_layer(layer)
            self.ffn_layer(layer)


def split_columns(w, n):
    k, m = w.shape
    return np.ascontiguousarray(w.reshape(k // P, P, m // n, n).transpose(2, 1, 0, 3)).reshape(m // n, P, -1)


def lay_out(inputs):
    a = {}
    a["consts"] = constant_columns()[1]
    a["x"] = inputs["x"][0]
    a["a_w_in"] = split_columns(inputs["a_w_in"][0], BANK)
    a["a_w_o"] = split_columns(inputs["a_w_o"][0], BANK)
    a["a_sinks"] = inputs["a_sinks"]
    a["b_w_down_q"] = split_columns(inputs["b_w_down"][0][:, :B_QR], B_QR)[0]
    a["b_w_down_kv"] = split_columns(inputs["b_w_down"][0][:, B_QR:], B_DOWN - B_QR)[0]
    a["b_w_uq"] = split_columns(inputs["b_w_uq"][0], BANK)
    a["b_w_ukv"] = split_columns(inputs["b_w_ukv"][0], BANK)
    a["b_w_o"] = split_columns(inputs["b_w_o"][0], BANK)
    a["b_q_norm"], a["b_kv_norm"] = inputs["b_q_norm"], inputs["b_kv_norm"]
    a["ctx"] = inputs["ctx_2"][0]
    a["c_columns"] = np.stack([inputs["c_2"][0], inputs["c_ctx_2"]]).reshape(2, KD, P).transpose(2, 1, 0)
    a["w_ada"] = np.concatenate([split_columns(w, BANK) for w in inputs["w_ada_2"]])
    a["b_ada"] = inputs["b_ada_2"]
    for n in ("norm_mix_g", "norm_ffn_g"):
        a[n] = inputs[n + "_2"].reshape(DEPTH, KD, P).transpose(0, 2, 1)
    w = inputs["w_in_2"]
    c = np.cumsum([0, QK, QK, GV, GLA_LR, GLA_LR, GV, 256, 256, 256, NA_H * DH, NA_H * DH, NA_H * DH])
    whole = lambda x: np.stack([split_columns(y, y.shape[1])[0] for y in x])
    a["w_qk"], a["w_v_lr"], a["w_r"] = (whole(w[:, :, c[i]:c[j]]) for i, j in ((0, 2), (2, 5), (5, 6)))
    a["w_nav"] = whole(w[:, :, c[11]:c[12]])
    a["w_cols"] = np.stack([split_columns(x, BANK) for x in w[:, :, c[6]:c[11]]])
    wb = [np.concatenate([inputs[f"gla_wg2_{d}_2"], inputs[f"gla_bg_{d}_2"][:, None, :]], 1) for d in ("fw", "bw")]
    a["gla_wg2"] = np.concatenate(wb, -1)
    a["gla_norm_g"] = inputs["gla_norm_g_2"]
    taps = lambda w, b: np.concatenate([w, b[:, None, :]], 1)
    a["sc_conv"] = taps(inputs["sc_conv_w_2"], inputs["sc_conv_b_2"]).reshape(DEPTH, 4, 2, P).transpose(0, 3, 2, 1)
    a["ffn_conv"] = taps(inputs["ffn_conv_w_2"], inputs["ffn_conv_b_2"]).reshape(
        DEPTH, 4, 2, NF, P).transpose(0, 4, 3, 2, 1)
    edge = GRID_W - NA_WIN
    a["rpb_padded"] = np.pad(inputs["na_rpb_2"], ((0, 0), (0, 0), (0, 0), (edge, edge)))[..., ::-1]
    a["w_out"] = np.stack([split_columns(x, BANK) for x in inputs["w_out_2"]])
    a["ffn_w_up"] = inputs["ffn_w_up_2"].reshape(DEPTH, KD, P, 2, NF, P).transpose(0, 4, 2, 1, 3, 5).reshape(
        DEPTH * NF, P, KD * 2 * P)
    a["ffn_w_down"] = np.stack([split_columns(w, BANK) for w in inputs["ffn_w_down_2"]])
    a["final_norm_g"] = inputs["final_norm_g_2"][None, :]
    router = np.concatenate([inputs["moe_w_group"], inputs["moe_w_expert"]], -1)
    a["router"] = np.stack([split_columns(w, w.shape[1])[0] for w in router])
    for n in ("gate", "up", "down"):
        w = inputs[f"moe_w_{n}"]
        l, e, k, m = w.shape
        a[f"moe_{n}"] = w.reshape(l * e, k // P, P, m).transpose(0, 2, 1, 3).reshape(l * e, P, -1)
    a["ln_g"], a["ln_b"] = inputs["ln_g"], inputs["ln_b"]
    return {k: np.ascontiguousarray(v) for k, v in a.items()}


def kernel(**inputs):
    import numpy as _np
    import concourse.bacc as _bacc
    from concourse.bass_utils import run_bass_kernel_spmd as _run

    nc = _bacc.Bacc("TRN2", target_bir_lowering=False, num_devices=1)
    arrays, ins = {}, {}
    for name, a in lay_out({k: _np.asarray(v) for k, v in inputs.items()}).items():
        arrays[f"in_{name}_dram"] = a
        ins[name] = nc.dram_tensor(f"in_{name}_dram", a.shape, mybir.dt.from_np(a.dtype), kind="ExternalInput").ap()
    out = nc.dram_tensor("out_0_dram", (T, DM), F32, kind="ExternalOutput").ap()
    Program(nc, ins, out).build()
    r = _run(nc, [arrays], core_ids=[0])
    return r.results[0]["out_0_dram"].reshape(1, T, DM)
```
